# Optimizing a Trainium2 kernel written in Bass

```python
import jax, jax.numpy as jnp
from jax import lax
import numpy as np

D_MODEL = 1024
BATCH = 1
SEQ = 256
DEPTH = 1
DEC_BATCH = 1
DEC_SEQ = 64
PAST_LEN = 256

CHUNK = 64
POOL_GROUPS = 4
POOL_WINDOWS = (2, 4, 8, 16)
POOL_MAX = 16
POOL_GDIM = D_MODEL // 8
POOL_WIDTH = POOL_GROUPS * POOL_GDIM
GMLP_HEADS = 4
GMLP_CHUNK = 128
GMLP_WIDTH = D_MODEL // 2
GMLP_HDIM = GMLP_WIDTH // GMLP_HEADS
IN_WIDTH = POOL_WIDTH + 2 * GMLP_WIDTH + 2 * D_MODEL
N_EXPERTS = 32
TOP_K = 4
D_FF = D_MODEL
SWIGLU_LIMIT = 7.0
SWIGLU_ALPHA = 1.702
EXPERT_BLOCK = 128
NORM_EPS = 1e-6
LN_EPS = 1e-5
N_MOD = 6

kernel_name = "pool_gmlp_moe_streaming_step"

def rms_norm(x, g):
    xf = x.astype(jnp.float32)
    y = xf * lax.rsqrt(jnp.mean(xf * xf, axis=-1, keepdims=True) + NORM_EPS)
    return (y * g.astype(jnp.float32)).astype(x.dtype)

def layer_norm(x, g, b):
    xf = x.astype(jnp.float32)
    mu = jnp.mean(xf, axis=-1, keepdims=True)
    var = jnp.mean(jnp.square(xf - mu), axis=-1, keepdims=True)
    y = (xf - mu) * lax.rsqrt(var + LN_EPS)
    return (y * g.astype(jnp.float32) + b.astype(jnp.float32)).astype(x.dtype)

def pool_mixer(a, hist, pos0, w_pool, s_pool):
    bsz, n_new, _ = a.shape
    n_hist = hist.shape[1]
    ext = jnp.concatenate([hist, a], axis=1).astype(jnp.float32)
    ext = ext.reshape(bsz, n_hist + n_new, POOL_GROUPS, POOL_GDIM)
    cs = jnp.cumsum(ext, axis=1)
    cs = jnp.concatenate([jnp.zeros((bsz, POOL_MAX, POOL_GROUPS, POOL_GDIM), jnp.float32), cs], axis=1)
    lo = POOL_MAX + n_hist
    pos = pos0 + jnp.arange(n_new)
    means = []
    for g, w in enumerate(POOL_WINDOWS):
        win_sum = cs[:, lo:lo + n_new, g] - cs[:, lo - w:lo - w + n_new, g]
        cnt = jnp.minimum(pos + 1, w).astype(jnp.float32)
        means.append(win_sum / cnt[None, :, None])
    mean = jnp.stack(means, axis=2)
    d = (mean - ext[:, n_hist:]).astype(a.dtype)
    y = jnp.einsum("blgc,gcd->blgd", d, w_pool)
    return y.reshape(bsz, n_new, POOL_WIDTH) * s_pool

def spatial_gate(u, v, w_s, b_s):
    bsz, n, _ = u.shape
    n_chunks = -(-n // GMLP_CHUNK)
    n_pad = n_chunks * GMLP_CHUNK
    vp = jnp.pad(v, ((0, 0), (0, n_pad - n), (0, 0)))
    vp = vp.reshape(bsz, n_chunks, GMLP_CHUNK, GMLP_HEADS, GMLP_HDIM)
    causal = jnp.tril(jnp.ones((GMLP_CHUNK, GMLP_CHUNK), dtype=bool))
    w_m = jnp.where(causal[None], w_s, jnp.zeros((), w_s.dtype))
    s = jnp.einsum("gqk,bnkgd->bnqgd", w_m, vp) + b_s.T[None, None, :, :, None]
    s = s.reshape(bsz, n_pad, GMLP_WIDTH)[:, :n]
    return u * s

def moe_ffn(h, w_router, b_router, w_up, b_up, w_down, b_down):
    n_tok, d = h.shape
    logits = (h @ w_router + b_router).astype(jnp.float32)
    top_vals, top_idx = lax.top_k(logits, TOP_K)
    gates = jax.nn.softmax(top_vals, axis=-1).astype(h.dtype)
    n_asg = n_tok * TOP_K
    e_flat = top_idx.reshape(n_asg)
    tok_flat = jnp.repeat(jnp.arange(n_tok, dtype=jnp.int32), TOP_K)
    g_flat = gates.reshape(n_asg)
    order = jnp.argsort(e_flat)
    e_sorted = e_flat[order]
    counts = jnp.bincount(e_flat, length=N_EXPERTS)
    padded = (counts + EXPERT_BLOCK - 1) // EXPERT_BLOCK * EXPERT_BLOCK
    starts = jnp.cumsum(counts) - counts
    pends = jnp.cumsum(padded)
    pstarts = pends - padded
    rank = jnp.arange(n_asg, dtype=jnp.int32) - starts[e_sorted]
    dest = pstarts[e_sorted] + rank
    n_blocks = -(-n_asg // EXPERT_BLOCK) + N_EXPERTS
    n_rows = n_blocks * EXPERT_BLOCK
    tok_buf = jnp.full((n_rows,), n_tok, jnp.int32).at[dest].set(tok_flat[order])
    g_buf = jnp.zeros((n_rows,), h.dtype).at[dest].set(g_flat[order])
    blk_start = jnp.arange(n_blocks, dtype=jnp.int32) * EXPERT_BLOCK
    blk_expert = jnp.minimum(jnp.searchsorted(pends, blk_start, side="right"), N_EXPERTS - 1)
    h_pad = jnp.concatenate([h, jnp.zeros((1, d), h.dtype)], axis=0)
    xb = h_pad[tok_buf].reshape(n_blocks, EXPERT_BLOCK, d)

    def expert_block(args):
        xe, e = args
        z = xe @ w_up[e] + b_up[e]
        zg, zl = z[:, :D_FF], z[:, D_FF:]
        zg = jnp.minimum(zg, SWIGLU_LIMIT)
        zl = jnp.clip(zl, -SWIGLU_LIMIT, SWIGLU_LIMIT)
        act = zg * jax.nn.sigmoid(SWIGLU_ALPHA * zg) * (zl + 1)
        return act @ w_down[e] + b_down[e]

    yb = lax.map(expert_block, (xb, blk_expert))
    y = jax.ops.segment_sum(yb.reshape(n_rows, d) * g_buf[:, None], tok_buf, num_segments=n_tok + 1)
    return y[:n_tok]

def trunk_layer(x, c, pool_hist, pos0, w_ada, b_ada, g_pre_mix, g_post_mix, g_pre_ffn, g_post_ffn,
                w_in, w_pool, s_pool, g_v, b_v, w_s, b_s, p_a, p_b, w_o,
                w_router, b_router, w_up, b_up, w_down, b_down):
    bsz, n, _ = x.shape
    mod = (jax.nn.silu(c) @ w_ada + b_ada).reshape(bsz, N_MOD, 1, D_MODEL)
    shift_m, scale_m, gate_m, shift_f, scale_f, gate_f = [mod[:, i] for i in range(N_MOD)]
    h = rms_norm(x, g_pre_mix) * (1 + scale_m) + shift_m
    proj = h @ w_in
    a, z, ga, gb = jnp.split(proj, [POOL_WIDTH, POOL_WIDTH + 2 * GMLP_WIDTH,
                                    POOL_WIDTH + 2 * GMLP_WIDTH + D_MODEL], axis=-1)
    y_a = pool_mixer(a, pool_hist, pos0, w_pool, s_pool)
    pool_state = jnp.concatenate([pool_hist, a], axis=1)[:, -(POOL_MAX - 1):]
    u, v = jnp.split(jax.nn.gelu(z, approximate=False), 2, axis=-1)
    v = layer_norm(v, g_v, b_v)
    y_b = spatial_gate(u, v, w_s, b_s)
    m = jax.nn.sigmoid(ga) * (y_a @ p_a) + jax.nn.sigmoid(gb) * (y_b @ p_b)
    x = x + gate_m * rms_norm(m @ w_o, g_post_mix)
    h = rms_norm(x, g_pre_ffn) * (1 + scale_f) + shift_f
    f = moe_ffn(h.reshape(bsz * n, D_MODEL), w_router, b_router, w_up, b_up, w_down, b_down)
    x = x + gate_f * rms_norm(f.reshape(bsz, n, D_MODEL), g_post_ffn)
    return x, pool_state, v

def setup_inputs(seed: int = 0) -> dict:
    key = jax.random.key(seed)
    k = jax.random.split(key, 32)

    def nrm(i, shape, scale):
        return jax.random.normal(k[i], shape, jnp.float32) * scale

    L = DEPTH
    return {
        "x_prompt": nrm(0, (BATCH, SEQ, D_MODEL), 1.0),
        "x_sample": nrm(1, (DEC_BATCH, DEC_SEQ, D_MODEL), 1.0),
        "cache_pool": nrm(2, (DEPTH, DEC_BATCH, POOL_MAX - 1, POOL_WIDTH), 1.0),
        "c_prompt": nrm(3, (BATCH, D_MODEL), 1.0),
        "c_sample": nrm(4, (DEC_BATCH, D_MODEL), 1.0),
        "w_ada": nrm(5, (L, D_MODEL, N_MOD * D_MODEL), 0.5 * D_MODEL ** -0.5),
        "b_ada": nrm(6, (L, N_MOD * D_MODEL), 0.02),
        "g_pre_mix": 1.0 + nrm(7, (L, D_MODEL), 0.05),
        "g_post_mix": 1.0 + nrm(8, (L, D_MODEL), 0.05),
        "g_pre_ffn": 1.0 + nrm(9, (L, D_MODEL), 0.05),
        "g_post_ffn": 1.0 + nrm(10, (L, D_MODEL), 0.05),
        "w_in": nrm(11, (L, D_MODEL, IN_WIDTH), D_MODEL ** -0.5),
        "w_pool": nrm(12, (L, POOL_GROUPS, POOL_GDIM, POOL_GDIM), POOL_GDIM ** -0.5),
        "s_pool": 1.0 + nrm(13, (L, POOL_WIDTH), 0.1),
        "g_v": 1.0 + nrm(14, (L, GMLP_WIDTH), 0.05),
        "b_v": nrm(15, (L, GMLP_WIDTH), 0.02),
        "w_s": nrm(16, (L, GMLP_HEADS, GMLP_CHUNK, GMLP_CHUNK), GMLP_CHUNK ** -0.5),
        "b_s": 1.0 + nrm(17, (L, GMLP_HEADS, GMLP_CHUNK), 0.05),
        "p_a": nrm(18, (L, POOL_WIDTH, D_MODEL), POOL_WIDTH ** -0.5),
        "p_b": nrm(19, (L, GMLP_WIDTH, D_MODEL), GMLP_WIDTH ** -0.5),
        "w_o": nrm(20, (L, D_MODEL, D_MODEL), D_MODEL ** -0.5),
        "w_router": nrm(21, (L, D_MODEL, N_EXPERTS), D_MODEL ** -0.5),
        "b_router": nrm(22, (L, N_EXPERTS), 0.01),
        "w_up": nrm(23, (L, N_EXPERTS, D_MODEL, 2 * D_FF), D_MODEL ** -0.5),
        "b_up": nrm(24, (L, N_EXPERTS, 2 * D_FF), 0.02),
        "w_down": nrm(25, (L, N_EXPERTS, D_FF, D_MODEL), D_FF ** -0.5),
        "b_down": nrm(26, (L, N_EXPERTS, D_MODEL), 0.02),
    }

def reference(x_prompt, x_sample, cache_pool, c_prompt, c_sample, w_ada, b_ada, g_pre_mix, g_post_mix,
              g_pre_ffn, g_post_ffn, w_in, w_pool, s_pool, g_v, b_v, w_s, b_s, p_a, p_b, w_o,
              w_router, b_router, w_up, b_up, w_down, b_down):
    xp, xs = x_prompt, x_sample
    pool_p, pool_s, v_s = [], [], []
    for l in range(DEPTH):
        lw = (w_ada[l], b_ada[l], g_pre_mix[l], g_post_mix[l], g_pre_ffn[l], g_post_ffn[l],
              w_in[l], w_pool[l], s_pool[l], g_v[l], b_v[l], w_s[l], b_s[l], p_a[l], p_b[l], w_o[l],
              w_router[l], b_router[l], w_up[l], b_up[l], w_down[l], b_down[l])
        no_hist = jnp.zeros((xp.shape[0], 0, POOL_WIDTH), xp.dtype)
        xp, sp, _ = trunk_layer(xp, c_prompt, no_hist, 0, *lw)
        xs, ss, vs = trunk_layer(xs, c_sample, cache_pool[l], PAST_LEN, *lw)
        pool_p.append(sp)
        pool_s.append(ss)
        v_s.append(vs)
    return (xp, xs, jnp.stack(pool_p), jnp.stack(pool_s), jnp.stack(v_s))


_drawn_inputs = setup_inputs


def setup_inputs(seed=0):
    import zlib

    import numpy as np

    out = dict(_drawn_inputs(seed))
    spreads = {}
    factors = {'g_post_ffn': 4.075,
     'b_v': 2.858,
     'b_s': 3.003,
     'b_router': 3.144,
     'b_up': 8.0,
     'b_down': 8.0}
    for name, (base, spread) in spreads.items():
        noise = np.random.default_rng([zlib.crc32(name.encode()), seed]).standard_normal(out[name].shape)
        drawn = base * np.exp(spread * noise) if base else spread * noise
        out[name] = __import__('jax').numpy.asarray(drawn.astype(out[name].dtype))
    for name, factor in factors.items():
        out[name] = (out[name] * factor).astype(out[name].dtype)
    return out
```

```python
import concourse.bass as bass
from concourse import mybir
from contextlib import ExitStack


def pool_gmlp_moe_streaming_step_kernel(
    nc: bass.Bass, x_prompt, x_sample, cache_pool, c_prompt, c_sample, w_ada, b_ada,
    g_pre_mix, g_post_mix, g_pre_ffn, g_post_ffn, w_in, w_pool, s_pool, g_v, b_v, w_s, b_s,
    p_a, p_b, w_o, w_router, b_router, w_up, b_up, w_down, b_down,
    y_prompt, y_sample, state_prompt, state_sample, state_v,
):
    f32, bf16, i32, u32 = mybir.dt.float32, mybir.dt.bfloat16, mybir.dt.int32, mybir.dt.uint32
    ALU, ACT, AX = mybir.AluOpType, mybir.ActivationFunctionType, mybir.AxisListType

    D = x_prompt.shape[2]
    KD = D // 128
    HALF = D // 2
    TILE_ROWS = [128, 128, 64]
    TILE_AT = [0, 128, 256]
    NT = len(TILE_ROWS)
    TOK = sum(TILE_ROWS)
    TILE_SEQ = [0, 0, 1]
    HIST = cache_pool.shape[2]
    PAD = HIST + 1
    PW = cache_pool.shape[3]
    NG = PW // 128
    E = w_router.shape[2]
    TOPK = 4
    F2 = w_up.shape[3]
    BLK = 64
    MAXB = TOK * TOPK // BLK + E
    LIMIT, ALPHA = 7.0, 1.702
    NORM_EPS, LN_EPS = 1e-6, 1e-5

    COL = 2048
    UPS = 16
    DNS = 4
    S0 = 6
    NS = UPS - S0
    chunks = []

    def w_cols(w, k, c, n):
        return w[0, :, c:c + n].rearrange("(k p) n -> p k n", p=128)

    for k in range(KD):
        chunks.append((("ada", 0, k), w_ada[0, k * 128:(k + 1) * 128, 0:COL], 1))
    for c in range(6):
        chunks.append((("in", c), w_cols(w_in, KD, c * 256, 256), KD))
    for q in (1, 2):
        for k in range(KD):
            chunks.append((("ada", q, k), w_ada[0, k * 128:(k + 1) * 128, q * COL:(q + 1) * COL], 1))
    for h in range(2):
        chunks.append((("pa", h), w_cols(p_a, NG, h * HALF, HALF), NG))
        chunks.append((("pb", h), w_cols(p_b, NG, h * HALF, HALF), NG))
        for c in (2 * h, 2 * h + 1):
            chunks.append((("in", 6 + c), w_cols(w_in, KD, (6 + c) * 256, 256), KD))
            chunks.append((("in", 10 + c), w_cols(w_in, KD, (10 + c) * 256, 256), KD))
    for c in range(4):
        chunks.append((("wo", c), w_o[0, c * 256:(c + 1) * 256, :].rearrange("(k p) n -> p k n", p=128), 2))
    NCH = len(chunks)
    AT = {name: n for n, (name, _, _) in enumerate(chunks)}
    slot_of = [S0 + n % NS for n in range(NCH)]
    arrivals = [16 * (n // NS + 1) for n in range(NCH)]
    mixer_uses = [0] * UPS
    for s in slot_of:
        mixer_uses[s] += 1

    x1_dram = nc.dram_tensor("x1_scratch", (TOK, D), f32).ap()
    rows_dram = nc.dram_tensor("expert_rows", (MAXB * BLK, D), f32).ap()

    up_rows = w_up.rearrange("l e d f -> (l e d) f")
    dn_rows = w_down.rearrange("l e f d -> (l e f) d")

    ctx = ExitStack()
    with ctx:
        def sb(name, shape, dt=f32):
            return ctx.enter_context(nc.sbuf_tensor(name, shape, dt))

        def sem(name):
            return ctx.enter_context(nc.semaphore(name))

        def v3(ap, **kw):
            return ap.rearrange("p (a b) -> p a b", **kw)

        UP = sb("up_ring", [128, UPS * COL])
        DN = sb("down_ring", [128, DNS * COL])
        X = sb("x_rows", [128, NT * D])
        H = sb("h_rows", [128, NT * D])
        B3 = sb("bias_parts", [128, 2 * 1536], bf16)
        MODF = sb("mod_last", [128, HALF])
        MOD01 = sb("mod_first", [128, 2, HALF])
        ident = sb("ident", [128, 128])
        ones = sb("ones", [128, 128])
        pick = sb("pick_row", [128, 2, 128])
        before = sb("before", [128, 128], bf16)
        onesb = sb("ones_bf16", [128, 128], bf16)
        WS = sb("w_s_rows", [128, NG * 128])
        WST = sb("w_s_T", [128, NG, 128])
        WP = sb("w_pool_sb", [128, NG, 128])
        WR = sb("w_router_sb", [128, KD, E])
        router_b = sb("router_bias", [128, E])
        modT = sb("mod_columns", [128, 4, 4, 2])
        iota_e = sb("iota_experts", [128, E])
        iota_b = sb("iota_block", [128, BLK])
        expert_id = sb("expert_id", [96, BLK])
        onehot_e = sb("onehot_expert", [96, 2, BLK], bf16)
        slot_f = sb("slot_f", [128, NT, TOPK])
        slot_i = sb("slot_i", [128, NT, TOPK], i32)
        gates = sb("gates", [128, NT, TOPK])
        table = sb("block_table", [1, 2 * E], i32)
        stat = sb("stat", [128, 6, 15])
        small = sb("small", [128, 32])
        dummy = sb("warm_cell", [128, 1])

        VAR, DEV, RST, TMPA, SUMA, SUMB = (stat[:, q, :] for q in range(6))
        MV = small[:, 0:6].rearrange("p (t a) -> p t a", t=NT)
        sP = small[:, 8:12]

        at = [0]

        def take(n):
            at[0] += n
            return UP[:, at[0] - n:at[0]]
        hT = v3(take(KD * TOK), a=KD)
        uT = v3(take(NG * TOK), a=NG)
        yaT = v3(take(NG * TOK), a=NG)
        ybT = v3(take(NG * TOK), a=NG)
        V_ = take(NT * PW)
        V = v3(V_, a=NT)
        brow = v3(take(3 * HALF), a=3)
        grow = v3(take(3 * HALF), a=3)
        CT = v3(take(KD * 32), a=KD)
        assert at[0] <= S0 * COL - D
        h2T = v3(UP[:, S0 * COL - D:S0 * COL], a=KD)
        csil = V_[0:2 * KD, 0:128]
        craw = V_[0:2 * KD, 128:256]
        hist = V_[0:HIST, 256:256 + PW]
        spr = V_[0:NG, 256 + PW:256 + PW + 128]
        EXTW = PAD + TILE_AT[2] + PAD + 64
        P_AT = PAD
        S_AT = PAD + TILE_AT[2] + PAD
        at[0] = 0

        def take_dn(n):
            at[0] += n
            return DN[:, at[0] - n:at[0]]
        mT = v3(take_dn(KD * TOK), a=KD)
        rest = at[0]
        SC = v3(take_dn(NG * EXTW), a=NG)
        SD = v3(take_dn(NG * EXTW), a=NG)
        EXT = v3(take_dn(NG * EXTW), a=NG)
        dT = v3(take_dn(NG * TOK), a=NG)
        rcnt = v3(take_dn(NG * PAD), a=NG)
        assert at[0] <= DNS * COL
        braw = DN[0:96, 0:3072]
        bmid = DN[0:96, 3072:3072 + 1536].bitcast(bf16)
        at[0] = rest
        SGA = v3(take_dn(2 * TOK), a=2)
        SGB = v3(take_dn(2 * TOK), a=2)
        TA = v3(take_dn(2 * TOK), a=2)
        TB = v3(take_dn(2 * TOK), a=2)
        at[0] = rest
        GM = [take_dn(D), take_dn(D)]
        PRE_A = [take_dn(D), take_dn(D)]
        PRE_B = take_dn(D)
        PRE_B1 = [take_dn(HALF), MOD01[:, 0, :]]
        assert at[0] <= DNS * COL
        rows96 = B3[96:97, :].bitcast(f32)
        bs_row, gv_row, bv_row = (rows96[:, q * PW:(q + 1) * PW] for q in range(3))
        OHW = TOPK * E
        one_hot = WS[:, 0:NT * OHW].rearrange("p (t k e) -> p t k e", t=NT, k=TOPK)
        top8 = WST[:, 0, 0:NT * 8].rearrange("p (t k) -> p t k", t=NT)
        idx8 = WST[:, 0, 32:32 + NT * 8].rearrange("p (t k) -> p t k", t=NT).bitcast(u32)
        idxf = WST[:, 0, 64:64 + NT * 8].rearrange("p (t k) -> p t k", t=NT)
        nblk = WST[:, 1, 0:E]
        incl = WST[:, 1, E:2 * E]
        first_b = WST[:, 1, 2 * E:3 * E]
        negm = WST[:, 1, 96:96 + NT]
        esum = WST[:, 1, 100:100 + NT]
        rsum = WST[:, 1, 104:104 + NT]
        zeros_e = WST[:, 2, 0:E]
        chosen = WST[:, 2, E:E + NT * E // 2].bitcast(bf16).rearrange("p (t e) -> p t e", t=NT)
        slot_te = WST[:, 3, 0:NT * E].rearrange("p (t e) -> p t e", t=NT)
        prod = WP[:, :, :].rearrange("p a b -> p (a b)")[:, 0:NT * OHW].rearrange(
            "p (t k e) -> p t k e", t=NT, k=TOPK)
        logits = v3(WS[:, NT * OHW:NT * OHW + NT * E], a=NT)

        same = MOD01[:, 1, 0:NT * BLK * TOPK // 2].bitcast(bf16).rearrange("p (t s k) -> p t s k", t=NT, s=BLK)
        sel = WP[:, :, :].rearrange("p a b -> p (a b)")[:, 0:NT * BLK].rearrange("p (t s) -> p t s", t=NT)
        xT_ = MOD01[:, 0, :]
        xT_blk = xT_.rearrange("p (c j s) -> p c j s", c=4, j=2)
        work = [X[:, q * HALF:(q + 1) * HALF] for q in range(6)]
        xg, zg, zl, sg, aT_, yb = work
        aT_blk = aT_.rearrange("p (c j s) -> p c j s", c=4, j=2)

        G = UP[:, 0:NT * TOPK * D].rearrange("p (t k d) -> p t k d", t=NT, k=TOPK)
        x1b = UP[:, 6 * COL:6 * COL + NT * D].rearrange("p (t d) -> p t d", t=NT)

        Xt = v3(X[:, :], a=NT)
        Ht = v3(H[:, :], a=NT)
        P = [ctx.enter_context(nc.psum_tensor(f"bank{q}", [128, HALF], f32)) for q in range(8)]

        def up_slot(s, pieces=1):
            ap = UP[:, s * COL:(s + 1) * COL]
            return ap if pieces == 1 else ap.rearrange("p (k n) -> p k n", k=pieces)

        def chunk(name):
            n = AT[name]
            return up_slot(slot_of[n], chunks[n][2])

        def dn_slot(q):
            return DN[:, q * COL:(q + 1) * COL].rearrange("p (k n) -> p k n", k=2)

        S = {}
        for name in (
            "c_loaded x_loaded rows0_loaded rows_loaded ws_loaded wp_loaded hist_loaded vec_loaded spool_loaded "
            "brt_loaded wr_loaded bias_loaded x1_loaded "
            "consts rows_clear ext_clear ws_masked bias_split pool_step "
            "c_sigmoid c_silu cT_ps cT wsT_ps wsT histT_ps hist_in spoolT_ps spool "
            "squared var_ready dev_ready dve_step mod_rows modT_ps modT h_rows hT_ps hT_sb h_cols shuffled "
            "a_sb u_sb v_sb gv_ps v_rows dT_sb ya_ps ya_sb st_ps st_sb s_ps yb_sb "
            "mix_ps gate_sb mix_sb wide_sb o_ps x1_rows h2_rows h2T_ps h2T_sb "
            "log_ps chosen_sb rank_ps neg_max exps route table_ready "
            "chunks_used down_used outs_stored v_stored state_stored rows_stored "
            "iota_next match sel_ready xg_ps xg_sb xt_ps xt_sb up_done zg_sb zl_sb zl1_sb sig_sb act_sb "
            "at_ps at_sb y_ps y_sb one_hot_e all_stored pad_clear zero_filled warm gf_ps gated f_rows f_done"
        ).split():
            S[name] = sem(name)
        up_full = [sem(f"up_full{s}") for s in range(UPS)]
        dn_full = [sem(f"down_full{s}") for s in range(DNS)]

        gathered = [sem(f"gathered{t}") for t in range(NT)]

        def arrived(eng, name):
            n = AT[name]
            eng.wait_ge(up_full[slot_of[n]], arrivals[n])

        def used(eng, name):
            eng.wait_ge(S["chunks_used"], AT[name] + 1)

        def expert_blocks(eng, body, per_expert=None):
            eng.wait_ge(S["table_ready"], 1)
            with eng.Fori(0, E // 2) as i:
                for p in range(2):
                    first = eng.value_load(table[0:1, bass.ds(i * 2 + p, 1)], min_val=1, max_val=MAXB)
                    last = eng.value_load(table[0:1, bass.ds(i * 2 + (p + E), 1)], min_val=1, max_val=MAXB)
                    if per_expert:
                        per_expert(i, p)
                    with eng.If(first < last):
                        with eng.Fori(first, last) as b:
                            body(b, i, p, False)
                    body(last, i, p, True)

        block = ctx.enter_context(nc.Block())

        @block.sync
        def _(sp):
            for s, c in ((0, c_prompt), (1, c_sample)):
                sp.dma_start(craw[s * KD:(s + 1) * KD, :], c[0:1, :].rearrange("a (k p) -> (a k) p", p=128)).then_inc(S["c_loaded"], 16)
            for n, (_, src, pieces) in enumerate(chunks):
                if n == KD:
                    sp.dma_start(WS[:, :].rearrange("p (g k) -> p g k", g=NG), w_s[0].rearrange("g q k -> q g k")).then_inc(S["ws_loaded"], 16)
                    sp.dma_start(WP[:, :, :], w_pool[0].rearrange("g c d -> c g d")).then_inc(S["wp_loaded"], 16)
                    sp.dma_start(hist, cache_pool[0, 0, :, :]).then_inc(S["hist_loaded"], 16)
                    sp.dma_start(spr, s_pool[0].rearrange("(g d) -> g d", g=NG)).then_inc(S["spool_loaded"], 16)
                    for row, vec in ((bs_row, b_s[0].rearrange("g q -> (g q)")), (gv_row, g_v[0]), (bv_row, b_v[0])):
                        sp.dma_start(row, vec.rearrange("(a n) -> a n", a=1)).then_inc(S["vec_loaded"], 16)
                if n == KD + 3:
                    sp.dma_start(router_b[:, :], b_router[0:1, :].broadcast_to([128, E])).then_inc(S["brt_loaded"], 16)
                    sp.dma_start(WR[:, :, :], w_router[0].rearrange("(k p) e -> p k e", p=128)).then_inc(S["wr_loaded"], 16)
                    for q in range(3):
                        sp.dma_start(braw[32 * q:32 * q + 32, 0:F2], b_up[0]).then_inc(S["bias_loaded"], 16)
                        sp.dma_start(braw[32 * q:32 * q + 32, F2:F2 + D], b_down[0]).then_inc(S["bias_loaded"], 16)
                if n >= NS:
                    sp.wait_ge(S["chunks_used"], n - NS + 1)
                sp.dma_start(up_slot(slot_of[n], pieces), src).then_inc(up_full[slot_of[n]], 16)

            def load_up(e, k, s):
                sp.dma_start(up_slot(s), up_rows[bass.ds(e * D + k * 128, 128), :]).then_inc(up_full[s], 16)

            def load_down(e, q):
                src = dn_rows[bass.ds(e * D + q * 256, 256), :].rearrange("(k p) n -> p k n", p=128)
                sp.dma_start(dn_slot(q), src).then_inc(dn_full[q], 16)

            sp.wait_ge(S["pad_clear"], 1)
            sp.dma_start(rows_dram[E * BLK:MAXB * BLK, :].rearrange("(n p) d -> p n d", p=BLK),
                         H[64:128, 2 * D:3 * D].unsqueeze(1).broadcast_to([BLK, MAXB - E, D])).then_inc(S["zero_filled"], 16)
            sp.wait_ge(S["chunks_used"], AT[("wo", 0)])
            sp.wait_ge(S["mod_rows"], 3)
            sp.wait_ge(S["v_stored"], 16)
            sp.wait_ge(S["yb_sb"], NG)
            for e, k in [(e, k) for e in (0, 1) for k in range(KD) if 8 * e + k != S0 - 1]:
                s = 8 * e + k
                if s >= S0:
                    sp.wait_ge(S["chunks_used"], max(n for n in range(NCH) if slot_of[n] == s) + 1)
                load_up(e, k, s)
            sp.wait_ge(S["h2_rows"], NT)
            for q in range(DNS):
                load_down(0, q)
            sp.wait_ge(S["log_ps"], NT)
            load_up(0, S0 - 1, S0 - 1)
            with sp.Fori(1, E // 2) as i:
                for p in range(2):
                    for k in range(KD):
                        sp.wait_ge(S["chunks_used"], i * 16 + (NCH + 8 * (p - 2) + k + 1))
                        load_up(i * 2 + p, k, 8 * p + k)
                    for q in range(DNS):
                        sp.wait_ge(S["down_used"], i * 8 + (4 * (p - 2) + q + 1))
                        load_down(i * 2 + (p - 1), q)
            for q in range(DNS):
                sp.wait_ge(S["down_used"], 4 * (E - 2) + q + 1)
                load_down(E - 1, q)
            sp.wait_ge(S["chunks_used"], NCH + 8 * (E - 1))
            sp.dma_start(x1b[:, 0:2, :], x1_dram[0:256, :].rearrange("(t p) d -> p t d", p=128)).then_inc(S["x1_loaded"], 16)
            sp.dma_start(x1b[0:64, 2, :], x1_dram[256:320, :]).then_inc(S["x1_loaded"], 16)
            for t in range(NT):
                sp.wait_ge(S["f_done"], t + 1)
                dst = y_prompt[0, t * 128:(t + 1) * 128, :] if t < 2 else y_sample[0, :, :]
                sp.dma_start(dst, G[0:TILE_ROWS[t], t, 0, :]).then_inc(S["outs_stored"], 16)
            sp.wait_ge(S["outs_stored"], 16 * NT)
            sp.wait_ge(S["state_stored"], 32)

        @block.gpsimd
        def _(pool):
            g = nc.gpsimd
            steps = [0]

            def link(ins):
                steps[0] += 1
                ins.then_inc(S["pool_step"], 1)
                pool.wait_ge(S["pool_step"], steps[0])

            link(g.memset(ident[:, :], 0.0))
            g.affine_select(out=ident[:, :], in_=ident[:, :], compare_op=ALU.not_equal, fill=1.0,
                            base=0, pattern=[[-1, 128]], channel_multiplier=1).then_inc(S["consts"], 1)
            pool.wait_ge(S["consts"], 1)
            link(g.memset(CT, 0.0))
            link(g.memset(stat[:, :, :], 1.0))
            link(g.memset(small[:, :], 1.0))
            link(g.memset(brow, 0.0))
            g.memset(grow, 1.0).then_inc(S["rows_clear"], 1)
            pool.wait_ge(S["rows_clear"], 1)
            for s in range(2):
                pool.dma_start(brow[s:97 + s:32, :, :], b_ada[0, :].rearrange("(q j f) -> j q f", q=3, j=4)).then_inc(S["rows0_loaded"], 16)
                pool.dma_start(grow[64 + s:97 + s:32, 0, :], g_pre_mix[0, :].rearrange("(j f) -> j f", j=2)).then_inc(S["rows0_loaded"], 16)
            for s in range(2):
                for gvec, q, p0 in ((g_post_mix, 1, 0), (g_pre_ffn, 2, 0), (g_post_ffn, 2, 64)):
                    pool.dma_start(grow[p0 + s:p0 + s + 33:32, q, :], gvec[0, :].rearrange("(j f) -> j f", j=2)).then_inc(S["rows_loaded"], 16)
            link(g.memset(pick[:, :, :], 0.0))
            for j in range(4):
                for s in range(2):
                    link(g.affine_select(out=pick[:, s, :], in_=pick[:, s, :], compare_op=ALU.not_equal,
                                         fill=1.0, base=-(32 * j + s), pattern=[[0, 128]],
                                         channel_multiplier=1))
            g.memset(ones[:, :], 1.0).then_inc(S["consts"], 1)
            pool.wait_ge(S["consts"], 2)
            pool.wait_ge(S["ws_loaded"], 16)
            w = WS[:, :].rearrange("p (g k) -> p g k", g=NG)
            g.affine_select(out=w, in_=w, compare_op=ALU.is_ge, fill=0.0, base=0,
                            pattern=[[0, NG], [-1, 128]], channel_multiplier=1).then_inc(S["ws_masked"], 1)
            pool.wait_ge(S["ws_masked"], 1)
            g.memset(H[64:128, 2 * D:3 * D], 0.0).then_inc(S["pad_clear"], 1)
            pool.wait_ge(S["pad_clear"], 1)
            for t in range(2):
                link(g.memset(EXT[:, :, 0:P_AT] if t == 0 else EXT[:, :, S_AT - PAD:S_AT], 0.0))
            for gr in range(NG):
                link(g.iota(rcnt[:, gr, :], pattern=[[1, PAD]], base=1, channel_multiplier=0,
                            allow_small_or_imprecise_dtypes=True))
                link(g.tensor_scalar(rcnt[:, gr, :], rcnt[:, gr, :], float(2 << gr), 0.0, ALU.min, ALU.max))
            g.memset(dummy[:, :], 0.0).then_inc(S["ext_clear"], 1)
            pool.wait_ge(S["ext_clear"], 1)
            link(g.memset(before[:, :], 0.0))
            link(g.affine_select(out=before[:, :], in_=before[:, :], compare_op=ALU.is_ge, fill=1.0,
                                 base=0, pattern=[[-1, 128]], channel_multiplier=1))
            link(g.memset(onesb[:, :], 1.0))
            link(g.memset(slot_f[:, :, :], 0.0))
            link(g.iota(iota_e[:, :], pattern=[[1, E]], base=0, channel_multiplier=0,
                        allow_small_or_imprecise_dtypes=True))
            for q in range(3):
                link(g.iota(expert_id[32 * q:32 * q + 32, :], pattern=[[0, BLK]], base=0, channel_multiplier=1,
                            allow_small_or_imprecise_dtypes=True))
            g.iota(iota_b[:, :], pattern=[[1, BLK]], base=BLK, channel_multiplier=0,
                   allow_small_or_imprecise_dtypes=True).then_inc(S["consts"], 1)
            pool.wait_ge(S["consts"], 3)
            M1 = MOD01[:, 1, :]
            pool.wait_ge(S["mix_sb"], KD)
            pool.wait_ge(S["mod_rows"], 3)
            wide = [[GM[s][:, 0:HALF], GM[s][:, HALF:D], PRE_A[s][:, 0:HALF], PRE_A[s][:, HALF:D]] +
                    ([PRE_B[:, 0:HALF], PRE_B[:, HALF:D]] if s == 0 else PRE_B1) for s in range(2)]
            rows = [M1[0:1], M1[32:33], MODF[0:1, :], MODF[32:33, :], M1[64:65], M1[96:97]]
            for s in range(2):
                if s == 1:
                    pool.wait_ge(S["shuffled"], 2)
                for dst, row in zip(wide[s], rows):
                    g.partition_broadcast(dst, row).then_inc(S["wide_sb"], 1)
                pool.wait_ge(S["wide_sb"], 6 * s + 6)
            pool.wait_ge(S["all_stored"], 1)
            for t in range(NT):
                r = TILE_ROWS[t]
                for k in range(TOPK):
                    g.indirect_dma_start(out=G[0:r, t, k, :], out_offset=None, in_=rows_dram,
                                         in_offset=bass.IndirectOffsetOnAxis(ap=slot_i[0:r, t, k:k + 1], axis=0),
                                         ).then_inc(gathered[t], 16)

        @block.scalar
        def _(act):
            a = nc.scalar
            act.dma_start(Xt[:, 0:2, :], x_prompt[0, :, :].rearrange("(t p) d -> p t d", p=128)).then_inc(S["x_loaded"], 16)
            act.dma_start(Xt[0:64, 2, :], x_sample[0, :, :]).then_inc(S["x_loaded"], 16)
            act.wait_ge(S["c_loaded"], 32)
            a.activation(csil, craw, ACT.Sigmoid).then_inc(S["c_sigmoid"], 1)
            act.wait_ge(S["x_loaded"], 32)
            act.wait_ge(S["rows_clear"], 1)
            for t, r in enumerate(TILE_ROWS):
                a.activation(Ht[0:r, t, :], Xt[0:r, t, :], ACT.Square, accum_out=SUMA[0:r, t:t + 1]).then_inc(S["squared"], 1)

            def root(q, c0, c1, r=128):
                act.wait_ge(S["var_ready"], q)
                a.activation(DEV[0:r, c0:c1], VAR[0:r, c0:c1], ACT.Sqrt).then_inc(S["dev_ready"], 1)
            root(1, 0, 3)
            for t, r in enumerate(TILE_ROWS):
                for q in range(2):
                    act.wait_ge(S["hT_ps"], 2 * t + q + 1)
                    a.activation(hT[:, 4 * q:4 * q + 4, TILE_AT[t]:TILE_AT[t] + r],
                                 v3(P[(2 * t + q + 2) % 8][:, :], a=4)[:, :, 0:r], ACT.Copy).then_inc(S["hT_sb"], 1)
            for q in range(NG):
                used(act, ("in", 2 + q // 2))
                a.activation(uT[:, q, :], P[4 + q][:, 0:TOK], ACT.Gelu).then_inc(S["u_sb"], 1)
            for t, r in enumerate(TILE_ROWS):
                used(act, ("in", 5))
                act.wait_ge(S["cT"], 1)
                act.wait_ge(S["hist_in"], 1)
                act.wait_ge(S["spool"], 1)
                a.activation(V[0:r, t, :], P[t][0:r, :], ACT.Gelu).then_inc(S["v_sb"], 1)
            root(2, 3, 6)
            act.wait_ge(S["v_rows"], NT)
            act.dma_start(state_v[0, 0, :, :], V[0:64, 2, :]).then_inc(S["v_stored"], 16)
            for s, dst in enumerate((state_prompt, state_sample)):
                act.wait_ge(S["st_sb"], s + 1)
                act.dma_start(dst[0, 0, :, :], H[0:HIST, s * PW:(s + 1) * PW]).then_inc(S["state_stored"], 16)
            for n in range(KD):
                act.wait_ge(S["mix_ps"], n + 1)
                if n >= 2:
                    act.wait_ge(S["mix_sb"], n - 1)
                bank = 4 * (n % 2)
                a.activation(SGA[:, n % 2, :], P[bank + 2][:, 0:TOK], ACT.Sigmoid).then_inc(S["gate_sb"], 1)
                a.activation(SGB[:, n % 2, :], P[bank + 3][:, 0:TOK], ACT.Sigmoid).then_inc(S["gate_sb"], 1)

            def h2_out(t):
                r = TILE_ROWS[t]
                for q in range(2):
                    act.wait_ge(S["h2T_ps"], 2 * t + q + 1)
                    a.activation(h2T[:, 4 * q:4 * q + 4, 0:r], v3(P[(6, 0, 2)[t] + q][:, :], a=4)[:, :, 0:r],
                                 ACT.Copy).then_inc(S["h2T_sb"], 1)
            for t, r in enumerate(TILE_ROWS):
                if t < NT - 1:
                    act.wait_ge(S["o_ps"], t + 1)
                else:
                    used(act, ("wo", 3))
                if t == 0:
                    act.wait_ge(S["state_stored"], 32)
                if t == NT - 1:
                    h2_out(0)
                for h in range(2):
                    a.activation(Ht[0:r, t, h * HALF:(h + 1) * HALF], P[2 * t + h][0:r, :], ACT.Square,
                                 accum_out=(SUMA if h == 0 else SUMB)[0:r, 6 + t:7 + t]).then_inc(S["squared"], 1)
                root(3 + 2 * t, 6 + t, 7 + t, r)
                act.wait_ge(S["x1_rows"], t + 1)
                a.activation(Ht[0:r, t, :], Xt[0:r, t, :], ACT.Square,
                             accum_out=SUMA[0:r, 9 + t:10 + t]).then_inc(S["squared"], 1)
                if t < 2:
                    act.dma_start(x1_dram[t * 128:(t + 1) * 128, :], Xt[:, t, :]).then_inc(S["rows_stored"], 16)
                else:
                    act.dma_start(x1_dram[256:320, :], Xt[0:64, 2, :]).then_inc(S["rows_stored"], 16)
                root(4 + 2 * t, 9 + t, 10 + t, r)
            for t in (1, 2):
                act.wait_ge(S["log_ps"], t)
                h2_out(t)
            for t, r in enumerate(TILE_ROWS):
                act.wait_ge(S["neg_max"], t + 1)
                a.activation(gates[0:r, t, :], top8[0:r, t, 0:TOPK], ACT.Exp, bias=negm[0:r, t:t + 1],
                             accum_out=esum[0:r, t:t + 1]).then_inc(S["exps"], 1)

            act.wait_ge(S["zero_filled"], 16)
            act.wait_ge(S["rows_stored"], 48)
            act.wait_ge(S["xg_ps"], 1)
            a.activation(xg, P[2][:, :], ACT.Copy).then_inc(S["xg_sb"], 1)
            act.wait_ge(S["ext_clear"], 1)
            a.activation(dummy[:, :], dummy[:, :], ACT.Sigmoid).then_inc(S["warm"], 1)
            act.wait_ge(S["warm"], 1)
            a.activation(dummy[:, :], dummy[:, :], ACT.Copy).then_inc(S["y_sb"], 1)
            act.wait_ge(S["y_sb"], 1)

            def body(b, i, p, last):
                act.wait_ge(S["warm"], b)
                a.activation(dummy[:, :], dummy[:, :], ACT.Sigmoid).then_inc(S["warm"], 1)
                act.wait_ge(S["zg_sb"], b)
                a.activation(sg, zg, ACT.Sigmoid, scale=ALPHA).then_inc(S["sig_sb"], 1)
                act.wait_ge(S["xg_ps"], b + 1)
                a.activation(xg, P[2][:, :], ACT.Copy).then_inc(S["xg_sb"], 1)
                act.wait_ge(S["y_ps"], b)
                act.wait_ge(S["rows_stored"], b * 32 + 16)
                a.activation(yb, P[5][:, :], ACT.Copy).then_inc(S["y_sb"], 1)
                act.wait_ge(S["y_sb"], b + 1)
                for j in range(2):
                    act.dma_start(rows_dram[bass.ds(b * BLK - BLK, BLK), j * HALF:(j + 1) * HALF],
                                  yb[j * BLK:(j + 1) * BLK, :]).then_inc(S["rows_stored"], 16)
            expert_blocks(act, body)
            end = act.value_load(table[0:1, 2 * E - 1:2 * E], min_val=1, max_val=MAXB)
            act.wait_ge(S["rows_stored"], end * 32 + 48)
            a.activation(dummy[:, :], dummy[:, :], ACT.Copy).then_inc(S["all_stored"], 1)
            for t, r in enumerate(TILE_ROWS):
                act.wait_ge(gathered[t], 16 * TOPK)
                a.activation(G[0:r, t, 0, :], G[0:r, t, 0, :], ACT.Copy, scale=gates[0:r, t, 0:1]).then_inc(S["gated"], 1)
                act.wait_ge(S["f_rows"], t + 1)
                a.activation(G[0:r, t, 1, :], G[0:r, t, 0, :], ACT.Square,
                             accum_out=SUMA[0:r, 12 + t:13 + t]).then_inc(S["squared"], 1)
                root(9 + t, 12 + t, 13 + t, r)

        @block.vector
        def _(dve):
            v = nc.vector
            steps = [0]

            def link(ins):
                steps[0] += 1
                ins.then_inc(S["dve_step"], 1)
                dve.wait_ge(S["dve_step"], steps[0])

            def inverse_root(q, c0, c1, r, eps, scale):
                var, dev, rst, tmp, suma = (z[0:r, c0:c1] for z in (VAR, DEV, RST, TMPA, SUMA))
                v.tensor_scalar(var, suma, scale, eps, ALU.mult, ALU.add).then_inc(S["var_ready"], 1)
                dve.wait_ge(S["dev_ready"], q)
                link(v.reciprocal(rst, dev))
                link(v.tensor_tensor(tmp, rst, rst, ALU.mult))
                link(v.tensor_tensor(tmp, tmp, var, ALU.mult))
                link(v.tensor_scalar(tmp, tmp, -0.5, 1.5, ALU.mult, ALU.add))
                link(v.tensor_tensor(rst, rst, tmp, ALU.mult))

            dve.wait_ge(S["c_sigmoid"], 1)
            v.tensor_tensor(csil, csil, craw, ALU.mult).then_inc(S["c_silu"], 1)
            dve.wait_ge(S["cT_ps"], 1)
            dve.wait_ge(S["rows_clear"], 1)
            v.tensor_copy(CT[:, :, 0:2], P[0][:, 0:2 * KD].rearrange("p (s k) -> p k s", s=2)).then_inc(S["cT"], 1)
            dve.wait_ge(S["squared"], 3)
            inverse_root(1, 0, 3, 128, NORM_EPS, 1.0 / D)
            for t, r in enumerate(TILE_ROWS):
                v.tensor_scalar(Ht[0:r, t, :], Xt[0:r, t, :], RST[0:r, t:t + 1], None, ALU.mult).then_inc(S["h_rows"], 1)

            def modulation(q, bank, dst):
                used(dve, ("ada", q, KD - 1))
                dve.wait_ge(S["rows0_loaded"], 64)
                if q:
                    dve.wait_ge(S["rows_loaded"], 96)
                link(v.tensor_tensor(dst, P[bank][:, :], brow[:, q, :], ALU.add))
                if q == 1:
                    ins = v.tensor_tensor(dst[0:64], dst[0:64], grow[0:64, q, :], ALU.mult)
                else:
                    p = slice(64, 128) if q == 0 else slice(0, 64)
                    ins = v.scalar_tensor_tensor(out=dst[p], in0=dst[p], scalar=1.0, in1=grow[p, q, :],
                                                 op0=ALU.add, op1=ALU.mult)
                if q == 2:
                    link(ins)
                    ins = v.tensor_tensor(dst[64:128], dst[64:128], grow[64:128, q, :], ALU.mult)
                ins.then_inc(S["mod_rows"], 1)
            modulation(0, 1, MOD01[:, 0, :])
            dve.wait_ge(S["modT_ps"], 1)
            v.tensor_copy(modT[:, :, :, :], P[0][:, :].rearrange("p (c j s) -> p c j s", c=4, j=4)[:, :, :, 0:2]).then_inc(S["modT"], 1)
            dve.wait_ge(S["modT"], 1)
            dve.wait_ge(S["hT_sb"], 2 * NT)
            for k in range(KD):
                c, j = k % 4, k // 4
                for s, (lo, hi) in enumerate(((0, 256), (256, TOK))):
                    v.tensor_scalar(hT[:, k, lo:hi], hT[:, k, lo:hi], modT[:, c, 2 + j, s:s + 1], modT[:, c, j, s:s + 1],
                                    ALU.mult, ALU.add).then_inc(S["h_cols"], 1)
            dve.wait_ge(S["wsT_ps"], 1)
            v.tensor_copy(WST[:, :, :].rearrange("p g q -> p (g q)"), P[1][:, :]).then_inc(S["wsT"], 1)
            dve.wait_ge(S["ext_clear"], 1)
            dve.wait_ge(S["histT_ps"], 1)
            v.tensor_copy(EXT[:, :, S_AT - HIST:S_AT], P[2][:, 0:NG * HIST].rearrange("p (g h) -> p g h", g=NG)).then_inc(S["hist_in"], 1)
            dve.wait_ge(S["spoolT_ps"], 1)
            v.tensor_copy(sP, P[3][:, 0:NG]).then_inc(S["spool"], 1)
            link(v.reciprocal(rcnt, rcnt))
            for q in range(NG):
                used(dve, ("in", q // 2))
                link(v.tensor_copy(EXT[:, q, P_AT:P_AT + 256], P[4 + q][:, 0:256]))
                v.tensor_copy(EXT[:, q, S_AT:S_AT + 64], P[4 + q][:, 256:TOK]).then_inc(S["a_sb"], 1)
            dve.wait_ge(S["a_sb"], NG)
            dve.wait_ge(S["bias_loaded"], 96)
            hi, mid = B3[0:96, :], bmid
            link(v.tensor_copy(hi, braw))
            link(v.tensor_tensor(braw, braw, hi, ALU.subtract))
            link(v.tensor_copy(mid, braw))
            link(v.tensor_copy(B3[32:64, :], mid[32:64, :]))
            link(v.tensor_tensor(braw, braw, mid, ALU.subtract))
            v.tensor_copy(B3[64:96, :], braw[64:96, :]).then_inc(S["bias_split"], 1)
            dve.wait_ge(S["bias_split"], 1)
            cur = EXT
            for lv in range(NG):
                nxt = SC if lv % 2 == 0 else SD
                sh, lo = 1 << lv, (2 << lv) - 1
                link(v.tensor_tensor(nxt[:, lv:NG, lo:EXTW], cur[:, lv:NG, lo:EXTW], cur[:, lv:NG, lo - sh:EXTW - sh], ALU.add))
                cur = nxt
            for q in range(NG):
                sums = SC if q % 2 == 0 else SD
                link(v.scalar_tensor_tensor(out=dT[:, q, 0:256], in0=sums[:, q, P_AT:P_AT + 256], scalar=1.0 / (2 << q),
                                            in1=EXT[:, q, P_AT:P_AT + 256], op0=ALU.mult, op1=ALU.subtract))
                link(v.scalar_tensor_tensor(out=dT[:, q, 256:TOK], in0=sums[:, q, S_AT:S_AT + 64], scalar=1.0 / (2 << q),
                                            in1=EXT[:, q, S_AT:S_AT + 64], op0=ALU.mult, op1=ALU.subtract))
                link(v.tensor_tensor(dT[:, q, 0:PAD], sums[:, q, P_AT:P_AT + PAD], rcnt[:, q, :], ALU.mult))
                v.tensor_tensor(dT[:, q, 0:PAD], dT[:, q, 0:PAD], EXT[:, q, P_AT:P_AT + PAD], ALU.subtract).then_inc(S["dT_sb"], 1)
            for q in range(NG):
                dve.wait_ge(S["ya_ps"], q + 1)
                v.tensor_scalar(yaT[:, q, :], P[6 + q % 2][:, 0:TOK], sP[:, q:q + 1], None, ALU.mult).then_inc(S["ya_sb"], 1)
            for t, r in enumerate(TILE_ROWS):
                dve.wait_ge(S["v_sb"], t + 1)
                link(v.bn_stats(SD[0:r, 0, 6 * t:6 * t + 6], V[0:r, t, :]))
                link(v.bn_aggr(MV[0:r, t, :], SD[0:r, 0, 6 * t:6 * t + 6]))
            link(v.tensor_copy(SUMA[:, 3:6], MV[:, :, 1]))
            inverse_root(2, 3, 6, 128, LN_EPS, 1.0)
            for t, r in enumerate(TILE_ROWS):
                dve.wait_ge(S["gv_ps"], 1)
                link(v.tensor_scalar(V[0:r, t, :], V[0:r, t, :], MV[0:r, t, 0:1], RST[0:r, 3 + t:4 + t], ALU.subtract, ALU.mult))
                link(v.tensor_tensor(V[0:r, t, :], V[0:r, t, :], P[3][0:r, :], ALU.mult))
                v.tensor_tensor(V[0:r, t, :], V[0:r, t, :], P[4][0:r, :], ALU.add).then_inc(S["v_rows"], 1)
            modulation(1, 5, MOD01[:, 1, :])
            modulation(2, 0, MODF[:, :])
            for s in range(2):
                dve.wait_ge(S["st_ps"], s + 1)
                v.tensor_copy(H[0:HIST, s * PW:(s + 1) * PW], P[1 + s][0:HIST, :]).then_inc(S["st_sb"], 1)
            for q in range(NG):
                dve.wait_ge(S["s_ps"], q + 1)
                dve.wait_ge(S["u_sb"], NG)
                v.tensor_tensor(ybT[:, q, :], uT[:, q, :], P[3 + q][:, 0:TOK], ALU.mult).then_inc(S["yb_sb"], 1)
            for n in range(KD):
                dve.wait_ge(S["gate_sb"], 2 * n + 2)
                bank, h = 4 * (n % 2), n % 2
                link(v.tensor_tensor(TA[:, h, :], SGA[:, h, :], P[bank][:, 0:TOK], ALU.mult))
                link(v.tensor_tensor(TB[:, h, :], SGB[:, h, :], P[bank + 1][:, 0:TOK], ALU.mult))
                v.tensor_tensor(mT[:, n, :], TA[:, h, :], TB[:, h, :], ALU.add).then_inc(S["mix_sb"], 1)
            dve.wait_ge(S["wide_sb"], 6)
            quad = [1] * 32
            for src in (MOD01[:, 1, :], MODF[0:64, :]):
                v.stream_shuffle(src, src, quad).then_inc(S["shuffled"], 1)
            for t, r in enumerate(TILE_ROWS):
                s = TILE_SEQ[t]
                if s == 1:
                    dve.wait_ge(S["wide_sb"], 12)
                dve.wait_ge(S["squared"], 3 + 3 * t + 2)
                link(v.tensor_tensor(SUMA[0:r, 6 + t:7 + t], SUMA[0:r, 6 + t:7 + t], SUMB[0:r, 6 + t:7 + t], ALU.add))
                inverse_root(3 + 2 * t, 6 + t, 7 + t, r, NORM_EPS, 1.0 / D)
                for h in range(2):
                    c = slice(h * HALF, (h + 1) * HALF)
                    link(v.scalar_tensor_tensor(out=Ht[0:r, t, c], in0=P[2 * t + h][0:r, :], scalar=RST[0:r, 6 + t:7 + t],
                                                in1=GM[s][0:r, c], op0=ALU.mult, op1=ALU.mult))
                v.tensor_tensor(Xt[0:r, t, :], Xt[0:r, t, :], Ht[0:r, t, :], ALU.add).then_inc(S["x1_rows"], 1)
                dve.wait_ge(S["squared"], 3 + 3 * t + 3)
                inverse_root(4 + 2 * t, 9 + t, 10 + t, r, NORM_EPS, 1.0 / D)
                link(v.scalar_tensor_tensor(out=Ht[0:r, t, :], in0=Xt[0:r, t, :], scalar=RST[0:r, 9 + t:10 + t],
                                            in1=PRE_A[s][0:r, :], op0=ALU.mult, op1=ALU.mult))
                for h in range(2):
                    c = slice(h * HALF, (h + 1) * HALF)
                    ins = v.tensor_tensor(Ht[0:r, t, c], Ht[0:r, t, c], (PRE_B1[h] if s else PRE_B[:, c])[0:r], ALU.add)
                    if h == 0:
                        link(ins)
                    else:
                        ins.then_inc(S["h2_rows"], 1)
            dve.wait_ge(S["consts"], 3)
            dve.wait_ge(S["brt_loaded"], 16)
            link(v.memset(chosen, 0.0))
            link(v.memset(zeros_e, 0.0))
            link(v.memset(one_hot, 0.0))
            for t, r in enumerate(TILE_ROWS):
                dve.wait_ge(S["log_ps"], t + 1)
                link(v.tensor_tensor(logits[0:r, t, :], P[(6, 7, 0)[t]][0:r, 0:E], router_b[0:r, :], ALU.add))
                link(v.max(top8[0:r, t, :], logits[0:r, t, :]))
                link(v.max_index(idx8[0:r, t, :], top8[0:r, t, :], logits[0:r, t, :]))
                v.tensor_scalar(negm[0:r, t:t + 1], top8[0:r, t, 0:1], -1.0, None, ALU.mult).then_inc(S["neg_max"], 1)
                link(v.tensor_copy(idxf[0:r, t, :], idx8[0:r, t, :]))
                link(v.tensor_tensor(one_hot[0:r, t, :, :], iota_e[0:r, :].unsqueeze(1).broadcast_to([r, TOPK, E]),
                                     idxf[0:r, t, 0:TOPK].unsqueeze(2).broadcast_to([r, TOPK, E]), ALU.is_equal))
                with nc.allow_low_precision("zeros and ones"):
                    v.tensor_reduce(chosen[0:r, t, :], one_hot[0:r, t, :, :].rearrange("p k e -> p e k"),
                                    AX.X, ALU.add).then_inc(S["chosen_sb"], 1)
            dve.wait_ge(S["rank_ps"], 1)
            cnt = P[1][:, NT * E:(NT + 1) * E]
            link(v.tensor_scalar(nblk, cnt, float(BLK), 1.0, ALU.is_gt, ALU.add))
            for m in range(2, -(-TOK // BLK)):
                link(v.scalar_tensor_tensor(out=nblk, in0=cnt, scalar=float(BLK * m), in1=nblk, op0=ALU.is_gt, op1=ALU.add))
            link(v.tensor_tensor_scan(incl, nblk, zeros_e, 0.0, ALU.add, ALU.add))
            link(v.tensor_tensor(first_b, incl, nblk, ALU.subtract))
            link(v.tensor_scalar(first_b, first_b, 1.0, None, ALU.add))
            link(v.tensor_copy(table[0:1, 0:E], first_b[0:1, :]))
            v.tensor_copy(table[0:1, E:2 * E], incl[0:1, :]).then_inc(S["table_ready"], 1)
            link(v.scalar_tensor_tensor(out=slot_te, in0=first_b.unsqueeze(1).broadcast_to([128, NT, E]), scalar=float(BLK),
                                        in1=v3(P[1][:, 0:NT * E], a=NT), op0=ALU.mult, op1=ALU.add))
            link(v.tensor_tensor(prod, one_hot, slot_te.unsqueeze(2).broadcast_to([128, NT, TOPK, E]), ALU.mult))
            link(v.tensor_reduce(slot_f[:, :, :], prod, AX.X, ALU.add))

            def match():
                v.tensor_tensor(same[:, :, :, :], iota_b[:, :].unsqueeze(1).unsqueeze(3).broadcast_to([128, NT, BLK, TOPK]),
                                slot_f[:, :, :].unsqueeze(2).broadcast_to([128, NT, BLK, TOPK]), ALU.is_equal).then_inc(S["match"], 1)

            def picks():
                v.tensor_reduce(sel[:, :, :], same[:, :, :, :], AX.X, ALU.add).then_inc(S["sel_ready"], 1)
            match()
            dve.wait_ge(S["match"], 1)
            picks()
            dve.wait_ge(S["sel_ready"], 1)
            for t, r in enumerate(TILE_ROWS):
                dve.wait_ge(S["exps"], t + 1)
                link(v.reciprocal(rsum[0:r, t:t + 1], esum[0:r, t:t + 1]))
                link(v.tensor_scalar(gates[0:r, t, :], gates[0:r, t, :], rsum[0:r, t:t + 1], None, ALU.mult))
            link(v.tensor_scalar(slot_i[:, :, :], slot_f[:, :, :], -float(BLK), None, ALU.add))

            dve.wait_ge(S["xt_ps"], 1)
            v.tensor_copy(xT_, P[3][:, :]).then_inc(S["xt_sb"], 1)

            def per_expert(i, p):
                v.tensor_scalar(onehot_e[:, p, :], expert_id[:, :], 0.0, None, ALU.is_equal).then_inc(S["one_hot_e"], 1)
                dve.wait_ge(S["one_hot_e"], i * 2 + (p + 1))
                v.tensor_scalar(expert_id[:, :], expert_id[:, :], -1.0, None, ALU.add)

            def body(b, i, p, last):
                dve.wait_ge(S["xg_ps"], b)
                v.tensor_scalar(iota_b[:, :], iota_b[:, :], float(BLK), None, ALU.add).then_inc(S["iota_next"], 1)
                dve.wait_ge(S["iota_next"], b)
                match()
                dve.wait_ge(S["match"], b + 1)
                picks()
                dve.wait_ge(S["up_done"], b)
                v.tensor_scalar(zg, P[0][:, :], LIMIT, None, ALU.min).then_inc(S["zg_sb"], 1)
                v.tensor_scalar(zl, P[1][:, :], LIMIT, -LIMIT, ALU.min, ALU.max).then_inc(S["zl_sb"], 1)
                dve.wait_ge(S["zg_sb"], b)
                dve.wait_ge(S["zl_sb"], b)
                v.scalar_tensor_tensor(out=zl, in0=zl, scalar=1.0, in1=zg, op0=ALU.add, op1=ALU.mult).then_inc(S["zl1_sb"], 1)
                dve.wait_ge(S["zl1_sb"], b)
                dve.wait_ge(S["sig_sb"], b)
                v.tensor_tensor(zg, zl, sg, ALU.mult).then_inc(S["act_sb"], 1)
                dve.wait_ge(S["at_ps"], b)
                v.tensor_copy(aT_, P[4][:, :]).then_inc(S["at_sb"], 1)
                dve.wait_ge(S["xt_ps"], b + 1)
                v.tensor_copy(xT_, P[3][:, :]).then_inc(S["xt_sb"], 1)
            expert_blocks(dve, body, per_expert)

            dve.wait_ge(S["x1_loaded"], 32)
            dve.wait_ge(S["gf_ps"], 1)
            for t, r in enumerate(TILE_ROWS):
                dve.wait_ge(gathered[t], 16 * TOPK)
                dve.wait_ge(S["gated"], t + 1)
                acc = G[0:r, t, 0, :]
                for k in range(1, TOPK):
                    ins = v.scalar_tensor_tensor(out=acc, in0=G[0:r, t, k, :], scalar=gates[0:r, t, k:k + 1], in1=acc,
                                                 op0=ALU.mult, op1=ALU.add)
                    if k < TOPK - 1:
                        link(ins)
                    else:
                        ins.then_inc(S["f_rows"], 1)
                dve.wait_ge(S["squared"], 12 + t + 1)
                inverse_root(9 + t, 12 + t, 13 + t, r, NORM_EPS, 1.0 / D)
                for h in range(2):
                    c = slice(h * HALF, (h + 1) * HALF)
                    bank = P[(6 if TILE_SEQ[t] == 0 else 0) + h]
                    link(v.scalar_tensor_tensor(out=acc[:, c], in0=acc[:, c], scalar=RST[0:r, 12 + t:13 + t],
                                                in1=bank[0:r, :], op0=ALU.mult, op1=ALU.mult))
                v.tensor_tensor(acc, acc, x1b[0:r, t, :], ALU.add).then_inc(S["f_done"], 1)

        @block.tensor
        def _(pe):
            mm, tr = nc.tensor.matmul, nc.tensor.transpose
            pe.wait_ge(S["consts"], 1)
            pe.wait_ge(S["c_silu"], 1)
            tr(P[0][:, 0:2 * KD], csil, ident[0:2 * KD, 0:2 * KD]).then_inc(S["cT_ps"], 1)

            def adaln(q, bank):
                for k in range(KD):
                    arrived(pe, ("ada", q, k))
                    w = chunk(("ada", q, k))
                    for j in range(4):
                        last = mm(P[bank][32 * j:32 * j + 32, :], CT[:, k, :], w[:, j * HALF:(j + 1) * HALF],
                                  start=(k == 0), stop=(k == KD - 1))
                    last.then_inc(S["chunks_used"], 1)

            def row_transposes(t, rows_ready, done, bank0):
                r = TILE_ROWS[t]
                pe.wait_ge(S[rows_ready], t + 1)
                for q in range(2):
                    bank = P[(bank0 + q) % 8]
                    for c in range(4):
                        last = tr(bank[:, c * 128:c * 128 + r], Ht[0:r, t, (4 * q + c) * 128:(4 * q + c + 1) * 128], ident[0:r, 0:r])
                    last.then_inc(S[done], 1)

            for t in range(NT):
                row_transposes(t, "h_rows", "hT_ps", 2 * t + 2)
            pe.wait_ge(S["cT"], 1)
            pe.wait_ge(S["hT_sb"], 2 * NT)
            adaln(0, 1)
            pe.wait_ge(S["mod_rows"], 1)
            for c in range(4):
                last = tr(P[0][:, c * 128:(c + 1) * 128], MOD01[:, 0, c * 128:(c + 1) * 128], ident[:, :])
            last.then_inc(S["modT_ps"], 1)
            pe.wait_ge(S["ws_masked"], 1)
            for q in range(NG):
                last = tr(P[1][:, q * 128:(q + 1) * 128], WS[:, q * 128:(q + 1) * 128], ident[:, :])
            last.then_inc(S["wsT_ps"], 1)
            pe.wait_ge(S["hist_loaded"], 16)
            for q in range(NG):
                last = tr(P[2][:, q * HIST:(q + 1) * HIST], hist[:, q * 128:(q + 1) * 128], ident[0:HIST, 0:HIST])
            last.then_inc(S["histT_ps"], 1)
            pe.wait_ge(S["spool_loaded"], 16)
            tr(P[3][:, 0:NG], spr, ident[0:NG, 0:NG]).then_inc(S["spoolT_ps"], 1)

            def columns(bank, name, pieces, off, rhs):
                w = chunk(name)
                for k in range(pieces):
                    if name == ("in", 0) and off == 0:
                        pe.wait_ge(S["h_cols"], 2 * k + 2)
                    last = mm(P[bank][:, 0:TOK], w[:, k, off:off + 128], rhs[:, k, :], start=(k == 0), stop=(k == pieces - 1))
                return last

            for q in range(NG):
                name = ("in", q // 2)
                arrived(pe, name)
                last = columns(4 + q, name, KD, (q % 2) * 128, hT)
                if q % 2:
                    last.then_inc(S["chunks_used"], 1)
            for q in range(NG):
                name = ("in", 2 + q // 2)
                arrived(pe, name)
                pe.wait_ge(S["a_sb"], q + 1)
                last = columns(4 + q, name, KD, (q % 2) * 128, hT)
                if q % 2:
                    last.then_inc(S["chunks_used"], 1)
            for c in range(2):
                name = ("in", 4 + c)
                arrived(pe, name)
                w = chunk(name)
                for t, r in enumerate(TILE_ROWS):
                    for k in range(KD):
                        last = mm(P[t][0:r, c * 256:(c + 1) * 256], hT[:, k, TILE_AT[t]:TILE_AT[t] + r], w[:, k, :],
                                  start=(k == 0), stop=(k == KD - 1))
                last.then_inc(S["chunks_used"], 1)
                if c == 0:
                    pe.wait_ge(S["wp_loaded"], 16)
                    pe.wait_ge(S["u_sb"], NG)
                    for q in range(NG):
                        pe.wait_ge(S["dT_sb"], q + 1)
                        if q >= 2:
                            pe.wait_ge(S["ya_sb"], q - 1)
                        mm(P[6 + q % 2][:, 0:TOK], WP[:, q, :], dT[:, q, :], start=True, stop=True).then_inc(S["ya_ps"], 1)
            pe.wait_ge(S["vec_loaded"], 48)
            pe.wait_ge(S["u_sb"], 1)
            mm(P[3][:, :], ones[96:97, :], gv_row, start=True, stop=True)
            mm(P[4][:, :], ones[96:97, :], bv_row, start=True, stop=True).then_inc(S["gv_ps"], 1)
            pe.wait_ge(S["u_sb"], NG)
            adaln(1, 5)
            pe.wait_ge(S["v_sb"], NT)
            adaln(2, 0)
            for s, c0 in enumerate((P_AT + 256 - HIST, S_AT + 64 - HIST)):
                for q in range(NG):
                    last = mm(P[1 + s][0:HIST, q * 128:(q + 1) * 128], EXT[:, q, c0:c0 + HIST], ident[:, :], start=True, stop=True)
                last.then_inc(S["st_ps"], 1)
            pe.wait_ge(S["v_rows"], NT)
            pe.wait_ge(S["mod_rows"], 2)
            pe.wait_ge(S["ya_sb"], NG)
            for q in range(NG):
                for t, r in enumerate(TILE_ROWS):
                    out = P[3 + q][:, TILE_AT[t]:TILE_AT[t] + r]
                    mm(out, ones[96:97, :], bs_row[:, q * 128:q * 128 + r], start=True, stop=False)
                    last = mm(out, V[0:r, t, q * 128:(q + 1) * 128], WST[0:r, q, 0:r], start=False, stop=True)
                last.then_inc(S["s_ps"], 1)
            pe.wait_ge(S["st_sb"], 2)
            pe.wait_ge(S["mod_rows"], 3)
            for n in range(KD):
                h, bank = n // 4, 4 * (n % 2)
                pe.wait_ge(S["yb_sb"], NG)
                if n >= 2:
                    pe.wait_ge(S["mix_sb"], n - 1)
                for name, to, rhs, pieces, off in (
                    (("in", 6 + n // 2), bank + 2, hT, KD, (n % 2) * 128), (("in", 10 + n // 2), bank + 3, hT, KD, (n % 2) * 128),
                    (("pa", h), bank, yaT, NG, (n % 4) * 128), (("pb", h), bank + 1, ybT, NG, (n % 4) * 128),
                ):
                    arrived(pe, name)
                    w = chunk(name)
                    for k in range(pieces):
                        last = mm(P[to][:, 0:TOK], w[:, k, off:off + 128], rhs[:, k, :], start=(k == 0), stop=(k == pieces - 1))
                        if n == 4 and to == bank + 2 and k == 0:
                            last.then_inc(S["chunks_used"], 6)
                last.then_inc(S["mix_ps"], 1)
            pe.wait_ge(S["mix_sb"], KD)

            def w_o_product(t):
                r = TILE_ROWS[t]
                for c in range(4):
                    arrived(pe, ("wo", c))
                    w = chunk(("wo", c))
                    for k in range(2):
                        for h in range(2):
                            last = mm(P[2 * t + h][0:r, :], mT[:, 2 * c + k, TILE_AT[t]:TILE_AT[t] + r],
                                      w[:, k, h * HALF:(h + 1) * HALF], start=(c + k == 0), stop=(c + k == 4))
                            if t == 0 and c + k + h == 0:
                                last.then_inc(S["chunks_used"], 6)
                    if t == NT - 1:
                        last.then_inc(S["chunks_used"], 1)
                if t < NT - 1:
                    last.then_inc(S["o_ps"], 1)

            def router(t):
                r = TILE_ROWS[t]
                pe.wait_ge(S["h2T_sb"], 2 * t + 2)
                for k in range(KD):
                    last = mm(P[(6, 7, 0)[t]][0:r, 0:E], h2T[:, k, 0:r], WR[:, k, :], start=(k == 0), stop=(k == KD - 1))
                last.then_inc(S["log_ps"], 1)
            pe.wait_ge(S["wr_loaded"], 16)
            w_o_product(0)
            w_o_product(1)
            row_transposes(0, "h2_rows", "h2T_ps", 6)
            w_o_product(2)
            router(0)
            row_transposes(1, "h2_rows", "h2T_ps", 0)
            router(1)
            row_transposes(2, "h2_rows", "h2T_ps", 2)
            router(2)
            pe.wait_ge(S["chosen_sb"], NT)
            pe.wait_ge(S["consts"], 3)
            for t in range(NT + 1):
                for u in range(min(t + 1, NT)):
                    last = mm(P[1][:, t * E:(t + 1) * E], (before if u == t else onesb)[:, :], chosen[:, u, :],
                              start=(u == 0), stop=(u == min(t, NT - 1)))
            last.then_inc(S["rank_ps"], 1)

            def wide(bank, src, j, s):
                return mm(P[bank][:, :], pick[32 * j:32 * j + 32, s, :], src[32 * j:32 * j + 32, :], start=True, stop=True)

            def gather():
                for t in range(NT):
                    for j in range(2):
                        last = mm(P[2][j * BLK:(j + 1) * BLK, :], sel[:, t, :], Ht[:, t, j * HALF:(j + 1) * HALF],
                                  start=(t == 0), stop=(t == NT - 1))
                last.then_inc(S["xg_ps"], 1)

            def four_transposes(bank, src, done):
                for c in range(4):
                    last = tr(P[bank][:, c * 128:(c + 1) * 128], src[:, c * 128:(c + 1) * 128], ident[:, :])
                last.then_inc(S[done], 1)

            pe.wait_ge(S["sel_ready"], 1)
            gather()
            pe.wait_ge(S["xg_sb"], 1)
            four_transposes(3, xg, "xt_ps")
            pe.wait_ge(S["bias_split"], 1)

            def body(b, i, p, last_block):
                pe.wait_ge(S["xt_sb"], b)
                for k in range(KD):
                    s = 8 * p + k
                    pe.wait_ge(up_full[s], i * 16 + 16 * (mixer_uses[s] + 1))
                    for half in range(2):
                        for j in range(2):
                            c0 = half * D + j * HALF
                            last = mm(P[half][j * BLK:(j + 1) * BLK, :], xT_blk[:, k % 4, k // 4, :],
                                      up_slot(s)[:, c0:c0 + HALF], start=(k == 0), stop=False)
                    if last_block:
                        last.then_inc(S["chunks_used"], 1)
                pe.wait_ge(S["one_hot_e"], i * 2 + (p + 1))
                for half in range(2):
                    for j in range(2):
                        c0 = half * D + j * HALF
                        last = mm(P[half][j * BLK:(j + 1) * BLK, :], onehot_e[:, p, :], B3[0:96, c0:c0 + HALF],
                                  start=False, stop=True)
                last.then_inc(S["up_done"], 1)
                pe.wait_ge(S["sel_ready"], b + 1)
                gather()
                pe.wait_ge(S["act_sb"], b)
                four_transposes(4, zg, "at_ps")
                pe.wait_ge(S["at_sb"], b)
                pe.wait_ge(S["y_sb"], b)
                for k in range(KD):
                    if k == 4:
                        pe.wait_ge(S["xg_sb"], b + 1)
                        four_transposes(3, xg, "xt_ps")
                    pe.wait_ge(dn_full[k // 2], i * 32 + 16 * (p + 1))
                    w = dn_slot(k // 2)
                    for j in range(2):
                        last = mm(P[5][j * BLK:(j + 1) * BLK, :], aT_blk[:, k % 4, k // 4, :],
                                  w[:, k % 2, j * HALF:(j + 1) * HALF], start=(k == 0), stop=False)
                    if last_block and k % 2:
                        last.then_inc(S["down_used"], 1)
                for j in range(2):
                    last = mm(P[5][j * BLK:(j + 1) * BLK, :], onehot_e[:, p, :], B3[0:96, F2 + j * HALF:F2 + (j + 1) * HALF],
                              start=False, stop=True)
                last.then_inc(S["y_ps"], 1)
            expert_blocks(pe, body)
            for s in range(2):
                for h in range(2):
                    last = wide((6, 0)[s] + h, MODF[:, :], 2 + h, s)
            last.then_inc(S["gf_ps"], 1)


_INS = ["x_prompt", "x_sample", "cache_pool", "c_prompt", "c_sample", "w_ada", "b_ada", "g_pre_mix", "g_post_mix",
        "g_pre_ffn", "g_post_ffn", "w_in", "w_pool", "s_pool", "g_v", "b_v", "w_s", "b_s", "p_a", "p_b", "w_o",
        "w_router", "b_router", "w_up", "b_up", "w_down", "b_down"]


def kernel(**inputs):
    import numpy as _np
    import concourse.bacc as _bacc
    from concourse import mybir as _mybir
    from concourse.bass_utils import run_bass_kernel_spmd as _run

    nc = _bacc.Bacc("TRN2", target_bir_lowering=False, num_devices=1)
    arrays, args = {}, []
    for name in _INS:
        a = _np.ascontiguousarray(inputs[name])
        arrays[f"in_{name}_dram"] = a
        args.append(nc.dram_tensor(f"in_{name}_dram", a.shape, _mybir.dt.from_np(a.dtype), kind="ExternalInput").ap())
    xp, xs, cache = (inputs[n].shape for n in ("x_prompt", "x_sample", "cache_pool"))
    outs = [xp, xs, (cache[0], xp[0], cache[2], cache[3]), cache, (cache[0], xs[0], xs[1], inputs["g_v"].shape[1])]
    for i, shape in enumerate(outs):
        args.append(nc.dram_tensor(f"out_{i}_dram", shape, _mybir.dt.from_np(_np.dtype("float32")), kind="ExternalOutput").ap())
    pool_gmlp_moe_streaming_step_kernel(nc, *args)
    r = _run(nc, [arrays], core_ids=[0])
    return tuple(r.results[0][f"out_{i}_dram"] for i in range(len(outs)))
```

```python
import concourse.bass as bass
from concourse import mybir
from contextlib import ExitStack


def pool_gmlp_moe_streaming_step_kernel(
    nc: bass.Bass, x_prompt, x_sample, cache_pool, c_prompt, c_sample, w_ada, b_ada,
    g_pre_mix, g_post_mix, g_pre_ffn, g_post_ffn, w_in, w_pool, s_pool, g_v, b_v, w_s, b_s,
    p_a, p_b, w_o, w_router, b_router, w_up, b_up, w_down, b_down,
    y_prompt, y_sample, state_prompt, state_sample, state_v,
):
    f32, bf16, i32, u32 = mybir.dt.float32, mybir.dt.bfloat16, mybir.dt.int32, mybir.dt.uint32
    ALU, ACT, AX = mybir.AluOpType, mybir.ActivationFunctionType, mybir.AxisListType

    D = x_prompt.shape[2]
    KD = D // 128
    HALF = D // 2
    TILE_ROWS = [128, 128, 64]
    TILE_AT = [0, 128, 256]
    NT = len(TILE_ROWS)
    LAST = (0, 2, 1)
    TOK = sum(TILE_ROWS)
    TILE_SEQ = [0, 0, 1]
    HIST = cache_pool.shape[2]
    PAD = HIST + 1
    PW = cache_pool.shape[3]
    NG = PW // 128
    E = w_router.shape[2]
    TOPK = 4
    F2 = w_up.shape[3]
    BLK = 64
    NQ = 128 // BLK
    QW = D // NQ
    PQ = QW // 128
    MAXB = TOK * TOPK // BLK + E
    LIMIT, ALPHA = 7.0, 1.702
    NORM_EPS, LN_EPS = 1e-6, 1e-5

    COL = 2048
    UPS = 16
    DNS = 4
    S0 = 6
    NS = UPS - S0
    chunks = []

    def w_cols(w, k, c, n):
        return w[0, :, c:c + n].rearrange("(k p) n -> p k n", p=128)

    for k in range(KD):
        chunks.append((("ada", 0, k), w_ada[0, k * 128:(k + 1) * 128, 0:COL], 1))
    ADA_AFTER = (0, 5, 3, 3, 3, 2)
    ada_left = [(q, k) for q in (1, 2) for k in range(KD)]
    ada_after = {}
    for c, n_ada in zip((4, 5, 0, 1, 2, 3), ADA_AFTER):
        chunks.append((("in", c), w_cols(w_in, KD, c * 256, 256), KD))
        ada_after[c], ada_left = ada_left[:n_ada], ada_left[n_ada:]
        for q, k in ada_after[c]:
            chunks.append((("ada", q, k), w_ada[0, k * 128:(k + 1) * 128, q * COL:(q + 1) * COL], 1))
    assert not ada_left
    for h in range(2):
        for c in (2 * h, 2 * h + 1):
            chunks.append((("in", 6 + c), w_cols(w_in, KD, (6 + c) * 256, 256), KD))
            chunks.append((("in", 10 + c), w_cols(w_in, KD, (10 + c) * 256, 256), KD))
            if c == 2 * h:
                chunks.append((("pa", h), w_cols(p_a, NG, h * HALF, HALF), NG))
                chunks.append((("pb", h), w_cols(p_b, NG, h * HALF, HALF), NG))
    for c in range(4):
        chunks.append((("wo", c), w_o[0, c * 256:(c + 1) * 256, :].rearrange("(k p) n -> p k n", p=128), 2))
    NCH = len(chunks)
    AT = {name: n for n, (name, _, _) in enumerate(chunks)}
    slot_of = [S0 + n % NS for n in range(NCH)]
    arrivals = [16 * (n // NS + 1) for n in range(NCH)]
    mixer_uses = [0] * UPS
    for s in slot_of:
        mixer_uses[s] += 1

    x1_dram = nc.dram_tensor("x1_scratch", (TOK, D), f32).ap()
    rows_dram = nc.dram_tensor("expert_rows", (MAXB * BLK, D), f32).ap()

    up_rows = w_up.rearrange("l e d f -> (l e d) f")
    dn_rows = w_down.rearrange("l e f d -> (l e f) d")

    ctx = ExitStack()
    with ctx:
        def sb(name, shape, dt=f32):
            return ctx.enter_context(nc.sbuf_tensor(name, shape, dt))

        def sem(name):
            return ctx.enter_context(nc.semaphore(name))

        def v3(ap, **kw):
            return ap.rearrange("p (a b) -> p a b", **kw)

        UP = sb("up_ring", [128, UPS * COL])
        DN = sb("down_ring", [128, DNS * COL])
        X = sb("x_rows", [128, NT * D])
        H = sb("h_rows", [128, NT * D])
        B3 = sb("bias_parts", [128, 2 * 1536], bf16)
        MODF = sb("mod_last", [128, HALF])
        MOD01 = sb("mod_first", [128, 2, HALF])
        ident = sb("ident", [128, 128])
        ones = sb("ones", [128, 128])
        pick = sb("pick_row", [128, 2, 128])
        before = sb("before", [128, 128], bf16)
        onesb = sb("ones_bf16", [128, 128], bf16)
        WS = sb("w_s_rows", [128, NG * 128])
        WST = sb("w_s_T", [128, NG, 128])
        WP = sb("w_pool_sb", [128, NG, 128])
        WR = sb("w_router_sb", [128, KD, E])
        router_b = sb("router_bias", [128, E])
        modT = sb("mod_columns", [128, 4, 4, 2])
        iota_e = sb("iota_experts", [128, E])
        iota_b = sb("iota_block", [128, BLK])
        MORE = TOK // BLK - (TOK % BLK == 0)
        full_blk = sb("full_blocks", [128, MORE])
        expert_id = sb("expert_id", [96, BLK])
        onehot_e = sb("onehot_expert", [96, 2, BLK], bf16)
        slot_f = sb("slot_f", [128, NT, TOPK])
        slot_i = sb("slot_i", [128, NT, TOPK], i32)
        gates = sb("gates", [128, NT, TOPK])
        table = sb("block_table", [1, 2 * E], i32)
        stat = sb("stat", [128, 6, 15])
        small = sb("small", [128, 32])
        dummy = sb("warm_cell", [128, 1])

        VAR, DEV, RST, TMPA, SUMA, SUMB = (stat[:, q, :] for q in range(6))
        TMPV = small[:, 12:30]
        MV = small[:, 0:6].rearrange("p (t a) -> p t a", t=NT)
        sP = small[:, 8:12]

        at = [0]

        def take(n):
            at[0] += n
            return UP[:, at[0] - n:at[0]]
        hT = v3(take(KD * TOK), a=KD)
        yaT = v3(take(NG * TOK), a=NG)
        ybT = v3(take(NG * TOK), a=NG)
        h2T = v3(take(D), a=KD)
        S1 = 3
        assert at[0] <= S1 * COL
        uT = v3(take(NG * TOK), a=NG)
        V_ = take(NT * PW)
        V = v3(V_, a=NT)
        brow = v3(take(3 * HALF), a=3)
        grow = v3(take(3 * HALF), a=3)
        CT = v3(take(KD * 32), a=KD)
        assert at[0] <= S0 * COL
        csil = V_[0:2 * KD, 0:128]
        craw = V_[0:2 * KD, 128:256]
        hist = V_[0:HIST, 256:256 + PW]
        spr = V_[0:NG, 256 + PW:256 + PW + 128]
        EXTW = PAD + TILE_AT[2] + PAD + 64
        P_AT = PAD
        S_AT = PAD + TILE_AT[2] + PAD
        at[0] = 0

        def take_dn(n):
            at[0] += n
            return DN[:, at[0] - n:at[0]]
        mT = v3(take_dn(KD * TOK), a=KD)
        rest = at[0]
        SC = v3(take_dn(NG * EXTW), a=NG)
        SD = v3(take_dn(NG * EXTW), a=NG)
        EXT = v3(take_dn(NG * EXTW), a=NG)
        dT = v3(take_dn(NG * TOK), a=NG)
        rcnt = v3(take_dn(NG * PAD), a=NG)
        assert at[0] <= DNS * COL
        braw = DN[0:96, 0:3072]
        bmid = DN[0:96, 3072:3072 + 1536].bitcast(bf16)
        at[0] = rest
        SGA = v3(take_dn(2 * TOK), a=2)
        SGB = v3(take_dn(2 * TOK), a=2)
        TA = v3(take_dn(2 * TOK), a=2)
        TB = v3(take_dn(2 * TOK), a=2)
        at[0] = rest
        GM, PRE_A = [take_dn(D)], [take_dn(D)]
        PRE_B = take_dn(D)
        D1 = 2
        assert at[0] >= D1 * COL
        GM.append(take_dn(D))
        PRE_A.append(take_dn(D))
        PRE_B1 = [take_dn(HALF), MOD01[:, 0, :]]
        assert at[0] <= DNS * COL
        rows96 = B3[96:97, :].bitcast(f32)
        bs_row, gv_row, bv_row = (rows96[:, q * PW:(q + 1) * PW] for q in range(3))
        OHW = TOPK * E
        one_hot = WS[:, 0:NT * OHW].rearrange("p (t k e) -> p t k e", t=NT, k=TOPK)
        top8 = WST[:, 0, 0:NT * 8].rearrange("p (t k) -> p t k", t=NT)
        idx8 = WST[:, 0, 32:32 + NT * 8].rearrange("p (t k) -> p t k", t=NT).bitcast(u32)
        idxf = WST[:, 0, 64:64 + NT * 8].rearrange("p (t k) -> p t k", t=NT)
        nblk = WST[:, 1, 0:E]
        incl = WST[:, 1, E:2 * E]
        first_b = WST[:, 1, 2 * E:3 * E]
        negm = WST[:, 1, 96:96 + NT]
        esum = WST[:, 1, 100:100 + NT]
        rsum = WST[:, 1, 104:104 + NT]
        ones_e = WST[:, 2, 0:E]
        chosen = WST[:, 2, E:E + NT * E // 2].bitcast(bf16).rearrange("p (t e) -> p t e", t=NT)
        slot_te = WST[:, 3, 0:NT * E].rearrange("p (t e) -> p t e", t=NT)
        prod = WP[:, :, :].rearrange("p a b -> p (a b)")[:, 0:NT * OHW].rearrange(
            "p (t k e) -> p t k e", t=NT, k=TOPK)
        over = WP[:, :, :].rearrange("p a b -> p (a b)")[:, 0:E * MORE].rearrange("p (e m) -> p e m", e=E)
        logits = v3(WS[:, NT * OHW:NT * OHW + NT * E], a=NT)

        same = MOD01[:, 1, 0:NT * BLK * TOPK // 2].bitcast(bf16).rearrange("p (t s k) -> p t s k", t=NT, s=BLK)
        sel = WP[:, :, :].rearrange("p a b -> p (a b)")[:, 0:NT * BLK].rearrange("p (t s) -> p t s", t=NT)
        xT_ = MOD01[:, 0, 0:QW]
        xT_blk = xT_.rearrange("p (c j s) -> p c j s", c=PQ, j=NQ)
        work = [X[:, q * QW:(q + 1) * QW] for q in range(6)]
        xg, zg, zl, sg, aT_, yb = work
        aT_blk = aT_.rearrange("p (c j s) -> p c j s", c=PQ, j=NQ)

        G = UP[:, 0:NT * TOPK * D].rearrange("p (t k d) -> p t k d", t=NT, k=TOPK)
        diag = H[:, 0:TOPK * 128].rearrange("p (k q) -> p k q", k=TOPK)
        x1b = UP[:, 6 * COL:6 * COL + NT * D].rearrange("p (t d) -> p t d", t=NT)

        Xt = v3(X[:, :], a=NT)
        Ht = v3(H[:, :], a=NT)
        P = [ctx.enter_context(nc.psum_tensor(f"bank{q}", [128, HALF], f32)) for q in range(8)]

        def o_bank(t, h):
            return P[2 * t + h][:, :] if t < NT - 1 else P[2 * t][64 * h:64 * h + 64, :]

        def up_slot(s, pieces=1):
            ap = UP[:, s * COL:(s + 1) * COL]
            return ap if pieces == 1 else ap.rearrange("p (k n) -> p k n", k=pieces)

        def chunk(name):
            n = AT[name]
            return up_slot(slot_of[n], chunks[n][2])

        def dn_slot(q):
            return DN[:, q * COL:(q + 1) * COL].rearrange("p (k n) -> p k n", k=2)

        S = {}
        for name in (
            "c_loaded x_loaded rows0_loaded rows_loaded ws_loaded wp_loaded hist_loaded vec_loaded spool_loaded "
            "brt_loaded wr_loaded bias_loaded x1_loaded "
            "consts rows_clear ext_clear ws_masked bias_split pool_step "
            "c_sigmoid c_silu cT_ps cT wsT_ps wsT histT_ps hist_in spoolT_ps spool "
            "squared var_ready dev_ready dve_step mod_rows modT_ps modT h_rows hT_ps hT_sb h_cols shuffled "
            "a_sb u_sb v_sb gv_ps v_rows dT_sb ya_ps ya_sb st_ps st_sb s_ps yb_sb "
            "mix_ps gate_sb mix_sb wide_sb o_ps x1_rows h2_rows h2T_ps h2T_sb "
            "log_ps chosen_sb rank_ps neg_max exps table_ready "
            "chunks_used down_used outs_stored v_stored state_stored rows_stored "
            "iota_next match sel_ready xg_ps xg_sb xt_ps xt_sb up_done zg_sb zl_sb zl1_sb sig_sb act_sb "
            "at_ps at_sb y_ps y_sb one_hot_e all_stored pad_clear warm gf_ps gated f_rows diagonals f1_ps f1_rows f_done"
        ).split():
            S[name] = sem(name)
        up_full = [sem(f"up_full{s}") for s in range(UPS)]
        dn_full = [sem(f"down_full{s}") for s in range(DNS)]
        gathered = [sem(f"gathered{t}") for t in range(NT)]

        def arrived(eng, name):
            n = AT[name]
            eng.wait_ge(up_full[slot_of[n]], arrivals[n])

        def used(eng, name):
            eng.wait_ge(S["chunks_used"], AT[name] + 1)

        def expert_blocks(eng, body, per_expert=None):
            eng.wait_ge(S["table_ready"], 1)
            with eng.Fori(0, E // 2) as i:
                for p in range(2):
                    first = eng.value_load(table[0:1, bass.ds(i * 2 + p, 1)], min_val=1, max_val=MAXB)
                    last = eng.value_load(table[0:1, bass.ds(i * 2 + (p + E), 1)], min_val=1, max_val=MAXB)
                    if per_expert:
                        per_expert(i, p)
                    with eng.If(first < last):
                        with eng.Fori(first, last) as b:
                            body(b, i, p, False)
                    body(last, i, p, True)

        block = ctx.enter_context(nc.Block())

        @block.sync
        def _(sp):
            for s, c in ((0, c_prompt), (1, c_sample)):
                sp.dma_start(craw[s * KD:(s + 1) * KD, :], c[0:1, :].rearrange("a (k p) -> (a k) p", p=128)).then_inc(S["c_loaded"], 16)

            def load_up(e, k, s):
                sp.dma_start(up_slot(s), up_rows[bass.ds(e * D + k * 128, 128), :]).then_inc(up_full[s], 16)

            def load_down(e, q):
                src = dn_rows[bass.ds(e * D + q * 256, 256), :].rearrange("(k p) n -> p k n", p=128)
                sp.dma_start(dn_slot(q), src).then_inc(dn_full[q], 16)

            def load_early(n):
                load_up(n // KD, n % KD, n)

            for n, (_, src, pieces) in enumerate(chunks):
                if n == KD:
                    sp.dma_start(WS[:, :].rearrange("p (g k) -> p g k", g=NG), w_s[0].rearrange("g q k -> q g k")).then_inc(S["ws_loaded"], 16)
                    sp.dma_start(WP[:, :, :], w_pool[0].rearrange("g c d -> c g d")).then_inc(S["wp_loaded"], 16)
                    sp.dma_start(hist, cache_pool[0, 0, :, :]).then_inc(S["hist_loaded"], 16)
                    sp.dma_start(spr, s_pool[0].rearrange("(g d) -> g d", g=NG)).then_inc(S["spool_loaded"], 16)
                    for row, vec in ((bs_row, b_s[0].rearrange("g q -> (g q)")), (gv_row, g_v[0]), (bv_row, b_v[0])):
                        sp.dma_start(row, vec.rearrange("(a n) -> a n", a=1)).then_inc(S["vec_loaded"], 16)
                if n == KD + 3:
                    sp.dma_start(router_b[:, :], b_router[0:1, :].broadcast_to([128, E])).then_inc(S["brt_loaded"], 16)
                    sp.dma_start(WR[:, :, :], w_router[0].rearrange("(k p) e -> p k e", p=128)).then_inc(S["wr_loaded"], 16)
                    for q in range(3):
                        sp.dma_start(braw[32 * q:32 * q + 32, 0:F2], b_up[0]).then_inc(S["bias_loaded"], 16)
                        sp.dma_start(braw[32 * q:32 * q + 32, F2:F2 + D], b_down[0]).then_inc(S["bias_loaded"], 16)
                if n == AT[("in", 9)]:
                    sp.wait_ge(S["mod_rows"], 3)
                    sp.wait_ge(S["v_stored"], 16)
                    sp.wait_ge(S["s_ps"], NG)
                    sp.wait_ge(S["yb_sb"], NG)
                    for s in range(S1, S0):
                        load_early(s)
                    sp.wait_ge(S["pad_clear"], 1)
                    sp.dma_start(rows_dram[E * BLK:MAXB * BLK, :].rearrange("(n p) d -> p n d", p=BLK),
                                 H[128 - BLK:128, 2 * D:3 * D].unsqueeze(1).broadcast_to([BLK, MAXB - E, D])).then_inc(S["rows_stored"], 16)
                if n >= NS:
                    sp.wait_ge(S["chunks_used"], n - NS + 1)
                sp.dma_start(up_slot(slot_of[n], pieces), src).then_inc(up_full[slot_of[n]], 16)

            last_use = {slot_of[n]: n for n in range(NCH)}
            by_release = sorted(last_use, key=lambda n: last_use[n])
            before_w_o = [n for n in by_release if last_use[n] < AT[("wo", 0)]]
            for n in before_w_o:
                sp.wait_ge(S["chunks_used"], last_use[n] + 1)
                load_early(n)
            sp.wait_ge(S["chunks_used"], AT[("wo", 0)])
            for n in range(S1 - 1):
                load_early(n)
            for n in by_release[len(before_w_o):]:
                sp.wait_ge(S["chunks_used"], last_use[n] + 1)
                load_early(n)
            for q in range(DNS):
                sp.wait_ge(S["h2_rows"], NT - 1 if q < D1 else NT)
                load_down(0, q)
            sp.wait_ge(S["log_ps"], NT)
            load_early(S1 - 1)

            def load_pair(i, downs):
                for p in range(2):
                    for k in range(KD):
                        sp.wait_ge(S["chunks_used"], i * 16 + (NCH + 8 * (p - 2) + k + 1))
                        load_up(i * 2 + p, k, 8 * p + k)
                    for d in downs[p]:
                        for q in range(DNS):
                            sp.wait_ge(S["down_used"], i * 8 + (4 * (d - 1) + q + 1))
                            load_down(i * 2 + d, q)
            with sp.Fori(1, E // 2 - 2) as i:
                load_pair(i, ((-1,), (0,)))
            load_pair(E // 2 - 2, ((-1, 0), (1,)))
            load_pair(E // 2 - 1, ((0,), (1,)))
            sp.wait_ge(S["chunks_used"], NCH + 8 * (E - 1))
            sp.dma_start(x1b[:, 0:2, :], x1_dram[0:256, :].rearrange("(t p) d -> p t d", p=128)).then_inc(S["x1_loaded"], 16)
            sp.dma_start(x1b[0:64, 2, :], x1_dram[256:320, :]).then_inc(S["x1_loaded"], 16)
            for i, t in enumerate(LAST):
                sp.wait_ge(S["f_done"], i + 1)
                dst = y_prompt[0, t * 128:(t + 1) * 128, :] if t < 2 else y_sample[0, :, :]
                sp.dma_start(dst, G[0:TILE_ROWS[t], t, 0, :]).then_inc(S["outs_stored"], 16)
            sp.wait_ge(S["outs_stored"], 16 * NT)
            sp.wait_ge(S["state_stored"], 32)

        @block.gpsimd
        def _(pool):
            g = nc.gpsimd
            steps = [0]

            def link(ins):
                steps[0] += 1
                ins.then_inc(S["pool_step"], 1)
                pool.wait_ge(S["pool_step"], steps[0])

            link(g.memset(ident[:, :], 0.0))
            g.affine_select(out=ident[:, :], in_=ident[:, :], compare_op=ALU.not_equal, fill=1.0,
                            base=0, pattern=[[-1, 128]], channel_multiplier=1).then_inc(S["consts"], 1)
            pool.wait_ge(S["consts"], 1)
            link(g.memset(CT, 0.0))
            link(g.memset(stat[:, :, :], 1.0))
            link(g.memset(small[:, :], 1.0))
            link(g.memset(brow, 0.0))
            g.memset(grow, 1.0).then_inc(S["rows_clear"], 1)
            pool.wait_ge(S["rows_clear"], 1)
            for s in range(2):
                pool.dma_start(brow[s:97 + s:32, :, :], b_ada[0, :].rearrange("(q j f) -> j q f", q=3, j=4)).then_inc(S["rows0_loaded"], 16)
                pool.dma_start(grow[64 + s:97 + s:32, 0, :], g_pre_mix[0, :].rearrange("(j f) -> j f", j=2)).then_inc(S["rows0_loaded"], 16)
            for s in range(2):
                for gvec, q, p0 in ((g_post_mix, 1, 0), (g_pre_ffn, 2, 0), (g_post_ffn, 2, 64)):
                    pool.dma_start(grow[p0 + s:p0 + s + 33:32, q, :], gvec[0, :].rearrange("(j f) -> j f", j=2)).then_inc(S["rows_loaded"], 16)
            link(g.memset(pick[:, :, :], 0.0))
            for j in range(4):
                for s in range(2):
                    link(g.affine_select(out=pick[:, s, :], in_=pick[:, s, :], compare_op=ALU.not_equal,
                                         fill=1.0, base=-(32 * j + s), pattern=[[0, 128]],
                                         channel_multiplier=1))
            g.memset(ones[:, :], 1.0).then_inc(S["consts"], 1)
            pool.wait_ge(S["consts"], 2)
            pool.wait_ge(S["ws_loaded"], 16)
            w = WS[:, :].rearrange("p (g k) -> p g k", g=NG)
            g.affine_select(out=w, in_=w, compare_op=ALU.is_ge, fill=0.0, base=0,
                            pattern=[[0, NG], [-1, 128]], channel_multiplier=1).then_inc(S["ws_masked"], 1)
            pool.wait_ge(S["ws_masked"], 1)
            g.memset(H[64:128, 2 * D:3 * D], 0.0).then_inc(S["pad_clear"], 1)
            pool.wait_ge(S["pad_clear"], 1)
            for t in range(2):
                link(g.memset(EXT[:, :, 0:P_AT] if t == 0 else EXT[:, :, S_AT - PAD:S_AT], 0.0))
            for gr in range(NG):
                link(g.iota(rcnt[:, gr, :], pattern=[[1, PAD]], base=1, channel_multiplier=0,
                            allow_small_or_imprecise_dtypes=True))
                link(g.tensor_scalar(rcnt[:, gr, :], rcnt[:, gr, :], float(2 << gr), 0.0, ALU.min, ALU.max))
            g.memset(dummy[:, :], 0.0).then_inc(S["ext_clear"], 1)
            pool.wait_ge(S["ext_clear"], 1)
            link(g.memset(before[:, :], 0.0))
            link(g.affine_select(out=before[:, :], in_=before[:, :], compare_op=ALU.is_ge, fill=1.0,
                                 base=0, pattern=[[-1, 128]], channel_multiplier=1))
            link(g.memset(onesb[:, :], 1.0))
            link(g.memset(slot_f[:, :, :], 0.0))
            link(g.iota(iota_e[:, :], pattern=[[1, E]], base=0, channel_multiplier=0,
                        allow_small_or_imprecise_dtypes=True))
            link(g.iota(full_blk[:, :], pattern=[[BLK, MORE]], base=BLK, channel_multiplier=0,
                        allow_small_or_imprecise_dtypes=True))
            for q in range(3):
                link(g.iota(expert_id[32 * q:32 * q + 32, :], pattern=[[0, BLK]], base=0, channel_multiplier=1,
                            allow_small_or_imprecise_dtypes=True))
            g.iota(iota_b[:, :], pattern=[[1, BLK]], base=BLK, channel_multiplier=0,
                   allow_small_or_imprecise_dtypes=True).then_inc(S["consts"], 1)
            pool.wait_ge(S["consts"], 3)
            M1 = MOD01[:, 1, :]
            pool.wait_ge(S["mix_sb"], KD)
            pool.wait_ge(S["mod_rows"], 3)
            wide = [[GM[s][:, 0:HALF], GM[s][:, HALF:D], PRE_A[s][:, 0:HALF], PRE_A[s][:, HALF:D]] +
                    ([PRE_B[:, 0:HALF], PRE_B[:, HALF:D]] if s == 0 else PRE_B1) for s in range(2)]
            rows = [M1[0:1], M1[32:33], MODF[0:1, :], MODF[32:33, :], M1[64:65], M1[96:97]]
            for s in range(2):
                if s == 1:
                    pool.wait_ge(S["shuffled"], 2)
                for dst, row in zip(wide[s], rows):
                    g.partition_broadcast(dst, row).then_inc(S["wide_sb"], 1)
                pool.wait_ge(S["wide_sb"], 6 * s + 6)
            pool.wait_ge(S["all_stored"], 1)
            for t in range(NT):
                r = TILE_ROWS[t]
                for k in range(TOPK):
                    g.indirect_dma_start(out=G[0:r, t, k, :], out_offset=None, in_=rows_dram,
                                         in_offset=bass.IndirectOffsetOnAxis(ap=slot_i[0:r, t, k:k + 1], axis=0),
                                         ).then_inc(gathered[t], 16)

        @block.scalar
        def _(act):
            a = nc.scalar
            act.dma_start(Xt[:, 0:2, :], x_prompt[0, :, :].rearrange("(t p) d -> p t d", p=128)).then_inc(S["x_loaded"], 16)
            act.dma_start(Xt[0:64, 2, :], x_sample[0, :, :]).then_inc(S["x_loaded"], 16)
            act.wait_ge(S["c_loaded"], 32)
            a.activation(csil, craw, ACT.Sigmoid).then_inc(S["c_sigmoid"], 1)
            act.wait_ge(S["x_loaded"], 32)
            act.wait_ge(S["rows_clear"], 1)
            for t, r in enumerate(TILE_ROWS):
                a.activation(Ht[0:r, t, :], Xt[0:r, t, :], ACT.Square, accum_out=SUMA[0:r, t:t + 1]).then_inc(S["squared"], 1)

            def root(q, c0, c1, r=128):
                act.wait_ge(S["var_ready"], q)
                a.activation(DEV[0:r, c0:c1], VAR[0:r, c0:c1], ACT.Sqrt).then_inc(S["dev_ready"], 1)
            root(1, 0, 3)
            for t, r in enumerate(TILE_ROWS):
                for q in range(2):
                    act.wait_ge(S["hT_ps"], 2 * t + q + 1)
                    a.activation(hT[:, 4 * q:4 * q + 4, TILE_AT[t]:TILE_AT[t] + r],
                                 v3(P[(2 * t + q + 2) % 8][:, :], a=4)[:, :, 0:r], ACT.Copy).then_inc(S["hT_sb"], 1)
            for t, r in enumerate(TILE_ROWS):
                used(act, ("in", 5))
                act.wait_ge(S["cT"], 1)
                act.wait_ge(S["hist_in"], 1)
                act.wait_ge(S["spool"], 1)
                for c in range(2):
                    if t == NT - 1:
                        a.activation(V[0:r, t, c * 256:(c + 1) * 256], P[t][64 * c:64 * c + 64, 0:256], ACT.Gelu).then_inc(S["v_sb"], 1)
                    elif c == 0:
                        a.activation(V[:, t, :], P[t][:, :], ACT.Gelu).then_inc(S["v_sb"], 1)
            root(2, 3, 6)
            act.wait_ge(S["v_rows"], NT)
            act.dma_start(state_v[0, 0, :, :], V[0:64, 2, :]).then_inc(S["v_stored"], 16)
            for q in range(NG):
                used(act, ("in", 2 + q // 2))
                a.activation(uT[:, q, :], P[4 + q][:, 0:TOK], ACT.Gelu).then_inc(S["u_sb"], 1)
            for s, dst in enumerate((state_prompt, state_sample)):
                act.wait_ge(S["st_sb"], s + 1)
                act.dma_start(dst[0, 0, :, :], H[0:HIST, s * PW:(s + 1) * PW]).then_inc(S["state_stored"], 16)
            for n in range(KD):
                act.wait_ge(S["mix_ps"], n + 1)
                if n >= 2:
                    act.wait_ge(S["mix_sb"], n - 1)
                bank = 4 * (n % 2)
                a.activation(SGA[:, n % 2, :], P[bank + 2][:, 0:TOK], ACT.Sigmoid).then_inc(S["gate_sb"], 1)
                a.activation(SGB[:, n % 2, :], P[bank + 3][:, 0:TOK], ACT.Sigmoid).then_inc(S["gate_sb"], 1)

            def h2_out(t):
                r = TILE_ROWS[t]
                for q in range(2):
                    act.wait_ge(S["h2T_ps"], 2 * t + q + 1)
                    a.activation(h2T[:, 4 * q:4 * q + 4, 0:r], v3(P[(6, 0, 2)[t] + q][:, :], a=4)[:, :, 0:r],
                                 ACT.Copy).then_inc(S["h2T_sb"], 1)
            for t, r in enumerate(TILE_ROWS):
                if t < NT - 1:
                    act.wait_ge(S["o_ps"], t + 1)
                else:
                    used(act, ("wo", 3))
                if t == 0:
                    act.wait_ge(S["state_stored"], 32)
                for h in range(2):
                    a.activation(Ht[0:r, t, h * HALF:(h + 1) * HALF], o_bank(t, h), ACT.Square,
                                 accum_out=(SUMA if h == 0 else SUMB)[0:r, 6 + t:7 + t]).then_inc(S["squared"], 1)
                root(3 + 2 * t, 6 + t, 7 + t, r)
                if t == NT - 1:
                    h2_out(0)
                act.wait_ge(S["x1_rows"], t + 1)
                a.activation(Ht[0:r, t, :], Xt[0:r, t, :], ACT.Square,
                             accum_out=SUMA[0:r, 9 + t:10 + t]).then_inc(S["squared"], 1)
                if t < 2:
                    act.dma_start(x1_dram[t * 128:(t + 1) * 128, :], Xt[:, t, :]).then_inc(S["rows_stored"], 16)
                else:
                    act.dma_start(x1_dram[256:320, :], Xt[0:64, 2, :]).then_inc(S["rows_stored"], 16)
                root(4 + 2 * t, 9 + t, 10 + t, r)
            for t in (1, 2):
                act.wait_ge(S["log_ps"], t)
                h2_out(t)
            for t, r in enumerate(TILE_ROWS):
                act.wait_ge(S["neg_max"], t + 1)
                a.activation(gates[0:r, t, :], top8[0:r, t, 0:TOPK], ACT.Exp, bias=negm[0:r, t:t + 1],
                             accum_out=esum[0:r, t:t + 1]).then_inc(S["exps"], 1)

            act.wait_ge(S["rows_stored"], 64)
            act.wait_ge(S["xg_ps"], 1)
            a.activation(xg, P[2][:, 0:QW], ACT.Copy).then_inc(S["xg_sb"], 1)
            act.wait_ge(S["ext_clear"], 1)
            a.activation(dummy[:, :], dummy[:, :], ACT.Sigmoid).then_inc(S["warm"], 1)
            act.wait_ge(S["warm"], 1)
            a.activation(dummy[:, :], dummy[:, :], ACT.Copy).then_inc(S["y_sb"], 1)
            act.wait_ge(S["y_sb"], 1)

            def body(b, i, p, last):
                act.wait_ge(S["warm"], b)
                a.activation(dummy[:, :], dummy[:, :], ACT.Sigmoid).then_inc(S["warm"], 1)
                act.wait_ge(S["zg_sb"], b)
                a.activation(sg, zg, ACT.Sigmoid, scale=ALPHA).then_inc(S["sig_sb"], 1)
                act.wait_ge(S["xg_ps"], b + 1)
                a.activation(xg, P[2][:, 0:QW], ACT.Copy).then_inc(S["xg_sb"], 1)
                act.wait_ge(S["y_ps"], b)
                act.wait_ge(S["rows_stored"], b * (16 * NQ) + (64 - 16 * NQ))
                a.activation(yb, P[5][:, 0:QW], ACT.Copy).then_inc(S["y_sb"], 1)
                act.wait_ge(S["y_sb"], b + 1)
                for j in range(NQ):
                    act.dma_start(rows_dram[bass.ds(b * BLK - BLK, BLK), j * QW:(j + 1) * QW],
                                  yb[j * BLK:(j + 1) * BLK, :]).then_inc(S["rows_stored"], 16)
            expert_blocks(act, body)
            end = act.value_load(table[0:1, 2 * E - 1:2 * E], min_val=1, max_val=MAXB)
            act.wait_ge(S["rows_stored"], end * (16 * NQ) + 64)
            a.activation(dummy[:, :], dummy[:, :], ACT.Copy).then_inc(S["all_stored"], 1)

            def gated(t):
                r = TILE_ROWS[t]
                act.wait_ge(gathered[t], 16 * TOPK)
                a.activation(G[0:r, t, 0, :], G[0:r, t, 0, :], ACT.Copy, scale=gates[0:r, t, 0:1]).then_inc(S["gated"], 1)
            gated(0)
            for i, t in enumerate(LAST):
                r = TILE_ROWS[t]
                if t == 1:
                    act.wait_ge(S["f1_ps"], 1)
                    for h in range(2):
                        a.activation(G[:, t, 0, h * HALF:(h + 1) * HALF], P[2 + h][:, :], ACT.Copy).then_inc(S["f1_rows"], 1)
                    act.wait_ge(S["f1_rows"], 2)
                else:
                    act.wait_ge(S["f_rows"], i + 1)
                a.activation(G[0:r, t, 1, :], G[0:r, t, 0, :], ACT.Square,
                             accum_out=SUMA[0:r, 12 + t:13 + t]).then_inc(S["squared"], 1)
                root(9 + i, 12 + t, 13 + t, r)
                if i == 0:
                    gated(LAST[1])

        @block.vector
        def _(dve):
            v = nc.vector
            steps = [0]

            def link(ins):
                steps[0] += 1
                ins.then_inc(S["dve_step"], 1)
                dve.wait_ge(S["dve_step"], steps[0])

            def inverse_root(q, c0, c1, r, eps, scale, meanwhile=None):
                var, dev, rst, tmp, suma = (z[0:r, c0:c1] for z in (VAR, DEV, RST, TMPA, SUMA))
                v.tensor_scalar(var, suma, scale, eps, ALU.mult, ALU.add).then_inc(S["var_ready"], 1)
                if meanwhile:
                    meanwhile()
                dve.wait_ge(S["dev_ready"], q)
                link(v.reciprocal(rst, dev))
                link(v.tensor_tensor(tmp, rst, rst, ALU.mult))
                link(v.tensor_tensor(tmp, tmp, var, ALU.mult))
                link(v.tensor_scalar(tmp, tmp, -0.5, 1.5, ALU.mult, ALU.add))
                link(v.tensor_tensor(rst, rst, tmp, ALU.mult))

            dve.wait_ge(S["c_sigmoid"], 1)
            v.tensor_tensor(csil, csil, craw, ALU.mult).then_inc(S["c_silu"], 1)
            dve.wait_ge(S["cT_ps"], 1)
            dve.wait_ge(S["rows_clear"], 1)
            v.tensor_copy(CT[:, :, 0:2], P[0][:, 0:2 * KD].rearrange("p (s k) -> p k s", s=2)).then_inc(S["cT"], 1)
            dve.wait_ge(S["squared"], 3)
            inverse_root(1, 0, 3, 128, NORM_EPS, 1.0 / D)
            for t, r in enumerate(TILE_ROWS):
                v.tensor_scalar(Ht[0:r, t, :], Xt[0:r, t, :], RST[0:r, t:t + 1], None, ALU.mult).then_inc(S["h_rows"], 1)

            def modulation(q, bank, dst):
                used(dve, ("ada", q, KD - 1))
                dve.wait_ge(S["rows0_loaded"], 64)
                if q:
                    dve.wait_ge(S["rows_loaded"], 96)
                link(v.tensor_tensor(dst, P[bank][:, :], brow[:, q, :], ALU.add))
                if q == 1:
                    ins = v.tensor_tensor(dst[0:64], dst[0:64], grow[0:64, q, :], ALU.mult)
                else:
                    p = slice(64, 128) if q == 0 else slice(0, 64)
                    ins = v.scalar_tensor_tensor(out=dst[p], in0=dst[p], scalar=1.0, in1=grow[p, q, :],
                                                 op0=ALU.add, op1=ALU.mult)
                if q == 2:
                    link(ins)
                    ins = v.tensor_tensor(dst[64:128], dst[64:128], grow[64:128, q, :], ALU.mult)
                ins.then_inc(S["mod_rows"], 1)
            modulation(0, 1, MOD01[:, 0, :])
            dve.wait_ge(S["modT_ps"], 1)
            v.tensor_copy(modT[:, :, :, :], P[0][:, :].rearrange("p (c j s) -> p c j s", c=4, j=4)[:, :, :, 0:2]).then_inc(S["modT"], 1)
            dve.wait_ge(S["modT"], 1)
            dve.wait_ge(S["hT_sb"], 2 * NT)
            for k in range(KD):
                c, j = k % 4, k // 4
                for s, (lo, hi) in enumerate(((0, 256), (256, TOK))):
                    v.tensor_scalar(hT[:, k, lo:hi], hT[:, k, lo:hi], modT[:, c, 2 + j, s:s + 1], modT[:, c, j, s:s + 1],
                                    ALU.mult, ALU.add).then_inc(S["h_cols"], 1)
            dve.wait_ge(S["wsT_ps"], 1)
            v.tensor_copy(WST[:, :, :].rearrange("p g q -> p (g q)"), P[4][:, :]).then_inc(S["wsT"], 1)
            dve.wait_ge(S["ext_clear"], 1)
            dve.wait_ge(S["histT_ps"], 1)
            v.tensor_copy(EXT[:, :, S_AT - HIST:S_AT], P[5][:, 0:NG * HIST].rearrange("p (g h) -> p g h", g=NG)).then_inc(S["hist_in"], 1)
            dve.wait_ge(S["spoolT_ps"], 1)
            v.tensor_copy(sP, P[6][:, 0:NG]).then_inc(S["spool"], 1)
            link(v.reciprocal(rcnt, rcnt))
            dve.wait_ge(S["bias_loaded"], 96)
            hi, mid = B3[0:96, :], bmid
            link(v.tensor_copy(hi, braw))
            link(v.tensor_tensor(braw, braw, hi, ALU.subtract))
            link(v.tensor_copy(mid, braw))
            link(v.tensor_copy(B3[32:64, :], mid[32:64, :]))
            link(v.tensor_tensor(braw, braw, mid, ALU.subtract))
            v.tensor_copy(B3[64:96, :], braw[64:96, :]).then_inc(S["bias_split"], 1)
            dve.wait_ge(S["bias_split"], 1)
            for t, r in enumerate(TILE_ROWS):
                dve.wait_ge(S["v_sb"], t + 1 if t < NT - 1 else NT + 1)
                link(v.bn_stats(TMPV[0:r, 6 * t:6 * t + 6], V[0:r, t, :]))
                link(v.bn_aggr(MV[0:r, t, :], TMPV[0:r, 6 * t:6 * t + 6]))
            link(v.tensor_copy(SUMA[:, 3:6], MV[:, :, 1]))
            inverse_root(2, 3, 6, 128, LN_EPS, 1.0)
            for t, r in enumerate(TILE_ROWS):
                dve.wait_ge(S["gv_ps"], 1)
                link(v.tensor_scalar(V[0:r, t, :], V[0:r, t, :], MV[0:r, t, 0:1], RST[0:r, 3 + t:4 + t], ALU.subtract, ALU.mult))
                link(v.tensor_tensor(V[0:r, t, :], V[0:r, t, :], P[0][0:r, :], ALU.mult))
                v.tensor_tensor(V[0:r, t, :], V[0:r, t, :], P[1][0:r, :], ALU.add).then_inc(S["v_rows"], 1)
            for q in range(NG):
                used(dve, ("in", q // 2))
                link(v.tensor_copy(EXT[:, q, P_AT:P_AT + 256], P[4 + q][:, 0:256]))
                v.tensor_copy(EXT[:, q, S_AT:S_AT + 64], P[4 + q][:, 256:TOK]).then_inc(S["a_sb"], 1)
            dve.wait_ge(S["a_sb"], NG)
            cur = EXT
            for lv in range(NG):
                nxt = SC if lv % 2 == 0 else SD
                sh, lo = 1 << lv, (2 << lv) - 1
                link(v.tensor_tensor(nxt[:, lv:NG, lo:EXTW], cur[:, lv:NG, lo:EXTW], cur[:, lv:NG, lo - sh:EXTW - sh], ALU.add))
                cur = nxt
            for q in range(NG):
                sums = SC if q % 2 == 0 else SD
                link(v.scalar_tensor_tensor(out=dT[:, q, 0:256], in0=sums[:, q, P_AT:P_AT + 256], scalar=1.0 / (2 << q),
                                            in1=EXT[:, q, P_AT:P_AT + 256], op0=ALU.mult, op1=ALU.subtract))
                link(v.scalar_tensor_tensor(out=dT[:, q, 256:TOK], in0=sums[:, q, S_AT:S_AT + 64], scalar=1.0 / (2 << q),
                                            in1=EXT[:, q, S_AT:S_AT + 64], op0=ALU.mult, op1=ALU.subtract))
                link(v.tensor_tensor(dT[:, q, 0:PAD], sums[:, q, P_AT:P_AT + PAD], rcnt[:, q, :], ALU.mult))
                v.tensor_tensor(dT[:, q, 0:PAD], dT[:, q, 0:PAD], EXT[:, q, P_AT:P_AT + PAD], ALU.subtract).then_inc(S["dT_sb"], 1)
            modulation(1, 3, MOD01[:, 1, :])
            for q in range(NG):
                dve.wait_ge(S["ya_ps"], q + 1)
                v.tensor_scalar(yaT[:, q, :], P[q % 2][:, 0:TOK], sP[:, q:q + 1], None, ALU.mult).then_inc(S["ya_sb"], 1)
            def y_b(q):
                dve.wait_ge(S["s_ps"], q + 1)
                dve.wait_ge(S["u_sb"], q + 1)
                v.tensor_tensor(ybT[:, q, :], uT[:, q, :], P[4 + q][:, 0:TOK], ALU.mult).then_inc(S["yb_sb"], 1)
            y_b(0)
            y_b(1)
            modulation(2, 2, MODF[:, :])
            for s in range(2):
                dve.wait_ge(S["st_ps"], s + 1)
                v.tensor_copy(H[0:HIST, s * PW:(s + 1) * PW], P[s][0:HIST, :]).then_inc(S["st_sb"], 1)
            y_b(2)
            y_b(3)
            for n in range(KD):
                dve.wait_ge(S["gate_sb"], 2 * n + 2)
                bank, h = 4 * (n % 2), n % 2
                link(v.tensor_tensor(TA[:, h, :], SGA[:, h, :], P[bank][:, 0:TOK], ALU.mult))
                link(v.tensor_tensor(TB[:, h, :], SGB[:, h, :], P[bank + 1][:, 0:TOK], ALU.mult))
                v.tensor_tensor(mT[:, n, :], TA[:, h, :], TB[:, h, :], ALU.add).then_inc(S["mix_sb"], 1)
            dve.wait_ge(S["wide_sb"], 6)
            quad = [1] * 32
            for src in (MOD01[:, 1, :], MODF[0:64, :]):
                v.stream_shuffle(src, src, quad).then_inc(S["shuffled"], 1)
            for t, r in enumerate(TILE_ROWS):
                s = TILE_SEQ[t]
                if s == 1:
                    dve.wait_ge(S["wide_sb"], 12)
                dve.wait_ge(S["squared"], 3 + 3 * t + 2)
                link(v.tensor_tensor(SUMA[0:r, 6 + t:7 + t], SUMA[0:r, 6 + t:7 + t], SUMB[0:r, 6 + t:7 + t], ALU.add))

                def scaled_o(h):
                    c = slice(h * HALF, (h + 1) * HALF)
                    p0 = 64 * h if t == NT - 1 else 0
                    return v.tensor_tensor(Ht[0:r, t, c], o_bank(t, h), GM[s][p0:p0 + r, c], ALU.mult)
                inverse_root(3 + 2 * t, 6 + t, 7 + t, r, NORM_EPS, 1.0 / D, lambda: (scaled_o(0), link(scaled_o(1))))
                v.scalar_tensor_tensor(out=Xt[0:r, t, :], in0=Ht[0:r, t, :], scalar=RST[0:r, 6 + t:7 + t],
                                       in1=Xt[0:r, t, :], op0=ALU.mult, op1=ALU.add).then_inc(S["x1_rows"], 1)
                dve.wait_ge(S["x1_rows"], t + 1)
                dve.wait_ge(S["squared"], 3 + 3 * t + 3)
                inverse_root(4 + 2 * t, 9 + t, 10 + t, r, NORM_EPS, 1.0 / D, lambda: link(
                    v.tensor_tensor(Ht[0:r, t, :], Xt[0:r, t, :], PRE_A[s][0:r, :], ALU.mult)))
                for h in range(2):
                    c = slice(h * HALF, (h + 1) * HALF)
                    ins = v.scalar_tensor_tensor(out=Ht[0:r, t, c], in0=Ht[0:r, t, c], scalar=RST[0:r, 9 + t:10 + t],
                                                 in1=(PRE_B1[h] if s else PRE_B[:, c])[0:r], op0=ALU.mult, op1=ALU.add)
                    if h == 0:
                        link(ins)
                    else:
                        ins.then_inc(S["h2_rows"], 1)
            dve.wait_ge(S["consts"], 3)
            dve.wait_ge(S["brt_loaded"], 16)
            link(v.memset(chosen, 0.0))
            link(v.memset(ones_e, 1.0))
            link(v.memset(one_hot, 0.0))
            for t, r in enumerate(TILE_ROWS):
                dve.wait_ge(S["log_ps"], t + 1)
                link(v.tensor_tensor(logits[0:r, t, :], P[(6, 7, 0)[t]][0:r, 0:E], router_b[0:r, :], ALU.add))
                link(v.max(top8[0:r, t, :], logits[0:r, t, :]))
                link(v.max_index(idx8[0:r, t, :], top8[0:r, t, :], logits[0:r, t, :]))
                v.tensor_scalar(negm[0:r, t:t + 1], top8[0:r, t, 0:1], -1.0, None, ALU.mult).then_inc(S["neg_max"], 1)
                link(v.tensor_copy(idxf[0:r, t, :], idx8[0:r, t, :]))
                link(v.tensor_tensor(one_hot[0:r, t, :, :], iota_e[0:r, :].unsqueeze(1).broadcast_to([r, TOPK, E]),
                                     idxf[0:r, t, 0:TOPK].unsqueeze(2).broadcast_to([r, TOPK, E]), ALU.is_equal))
                with nc.allow_low_precision("zeros and ones"):
                    v.tensor_reduce(chosen[0:r, t, :], one_hot[0:r, t, :, :].rearrange("p k e -> p e k"),
                                    AX.X, ALU.add).then_inc(S["chosen_sb"], 1)
            dve.wait_ge(S["rank_ps"], 1)
            cnt = P[1][:, NT * E:(NT + 1) * E]
            link(v.tensor_tensor(over, cnt.unsqueeze(2).broadcast_to([128, E, MORE]),
                                 full_blk[:, :].unsqueeze(1).broadcast_to([128, E, MORE]), ALU.is_gt))
            link(v.tensor_reduce(nblk, over, AX.X, ALU.add))
            link(v.tensor_tensor_scan(incl, nblk, ones_e, 0.0, ALU.add, ALU.add))
            link(v.tensor_tensor(first_b, incl, nblk, ALU.subtract))
            link(v.tensor_copy(table[0:1, 0:E], first_b[0:1, :]))
            v.tensor_copy(table[0:1, E:2 * E], incl[0:1, :]).then_inc(S["table_ready"], 1)
            link(v.scalar_tensor_tensor(out=slot_te, in0=first_b.unsqueeze(1).broadcast_to([128, NT, E]), scalar=float(BLK),
                                        in1=v3(P[1][:, 0:NT * E], a=NT), op0=ALU.mult, op1=ALU.add))
            link(v.tensor_tensor(prod, one_hot, slot_te.unsqueeze(2).broadcast_to([128, NT, TOPK, E]), ALU.mult))
            link(v.tensor_reduce(slot_f[:, :, :], prod, AX.X, ALU.add))

            def match():
                v.tensor_tensor(same[:, :, :, :], iota_b[:, :].unsqueeze(1).unsqueeze(3).broadcast_to([128, NT, BLK, TOPK]),
                                slot_f[:, :, :].unsqueeze(2).broadcast_to([128, NT, BLK, TOPK]), ALU.is_equal).then_inc(S["match"], 1)

            def picks():
                v.tensor_reduce(sel[:, :, :], same[:, :, :, :], AX.X, ALU.add).then_inc(S["sel_ready"], 1)
            match()
            dve.wait_ge(S["match"], 1)
            picks()
            dve.wait_ge(S["sel_ready"], 1)
            for t, r in enumerate(TILE_ROWS):
                dve.wait_ge(S["exps"], t + 1)
                link(v.reciprocal(rsum[0:r, t:t + 1], esum[0:r, t:t + 1]))
                link(v.tensor_scalar(gates[0:r, t, :], gates[0:r, t, :], rsum[0:r, t:t + 1], None, ALU.mult))
            link(v.tensor_scalar(slot_i[:, :, :], slot_f[:, :, :], -float(BLK), None, ALU.add))

            dve.wait_ge(S["xt_ps"], 1)
            v.tensor_copy(xT_, P[3][:, 0:QW]).then_inc(S["xt_sb"], 1)

            def per_expert(i, p):
                v.tensor_scalar(onehot_e[:, p, :], expert_id[:, :], 0.0, None, ALU.is_equal).then_inc(S["one_hot_e"], 1)
                dve.wait_ge(S["one_hot_e"], i * 2 + (p + 1))
                v.tensor_scalar(expert_id[:, :], expert_id[:, :], -1.0, None, ALU.add)

            def body(b, i, p, last):
                dve.wait_ge(S["xg_ps"], b)
                v.tensor_scalar(iota_b[:, :], iota_b[:, :], float(BLK), None, ALU.add).then_inc(S["iota_next"], 1)
                dve.wait_ge(S["iota_next"], b)
                match()
                dve.wait_ge(S["match"], b + 1)
                picks()
                dve.wait_ge(S["up_done"], b)
                v.tensor_scalar(zg, P[0][:, 0:QW], LIMIT, None, ALU.min).then_inc(S["zg_sb"], 1)
                v.tensor_scalar(zl, P[1][:, 0:QW], LIMIT, -LIMIT, ALU.min, ALU.max).then_inc(S["zl_sb"], 1)
                dve.wait_ge(S["zg_sb"], b)
                dve.wait_ge(S["zl_sb"], b)
                v.scalar_tensor_tensor(out=zl, in0=zl, scalar=1.0, in1=zg, op0=ALU.add, op1=ALU.mult).then_inc(S["zl1_sb"], 1)
                dve.wait_ge(S["zl1_sb"], b)
                dve.wait_ge(S["sig_sb"], b)
                v.tensor_tensor(zg, zl, sg, ALU.mult).then_inc(S["act_sb"], 1)
                dve.wait_ge(S["at_ps"], b)
                v.tensor_copy(aT_, P[4][:, 0:QW]).then_inc(S["at_sb"], 1)
                dve.wait_ge(S["xt_ps"], b + 1)
                v.tensor_copy(xT_, P[3][:, 0:QW]).then_inc(S["xt_sb"], 1)
            expert_blocks(dve, body, per_expert)

            for k in range(TOPK):
                v.tensor_scalar(diag[:, k, :], ident[:, :], gates[:, 1, k:k + 1], None, ALU.mult).then_inc(S["diagonals"], 1)
            dve.wait_ge(S["x1_loaded"], 32)
            dve.wait_ge(S["gf_ps"], 1)

            def weighted(t, i):
                r = TILE_ROWS[t]
                dve.wait_ge(gathered[t], 16 * TOPK)
                dve.wait_ge(S["gated"], i + 1)
                acc = G[0:r, t, 0, :]
                for k in range(1, TOPK):
                    ins = v.scalar_tensor_tensor(out=acc, in0=G[0:r, t, k, :], scalar=gates[0:r, t, k:k + 1], in1=acc,
                                                 op0=ALU.mult, op1=ALU.add)
                    if k < TOPK - 1:
                        link(ins)
                    else:
                        ins.then_inc(S["f_rows"], 1)
            for i, t in enumerate(LAST):
                r = TILE_ROWS[t]
                if t != 1:
                    weighted(t, i)
                acc = G[0:r, t, 0, :]
                dve.wait_ge(S["squared"], 12 + i + 1)

                def scaled_f():
                    for h in range(2):
                        c = slice(h * HALF, (h + 1) * HALF)
                        bank = P[(6 if TILE_SEQ[t] == 0 else 0) + h]
                        link(v.tensor_tensor(acc[:, c], acc[:, c], bank[0:r, :], ALU.mult))
                inverse_root(9 + i, 12 + t, 13 + t, r, NORM_EPS, 1.0 / D, scaled_f)
                v.scalar_tensor_tensor(out=acc, in0=acc, scalar=RST[0:r, 12 + t:13 + t], in1=x1b[0:r, t, :],
                                       op0=ALU.mult, op1=ALU.add).then_inc(S["f_done"], 1)

        @block.tensor
        def _(pe):
            mm, tr = nc.tensor.matmul, nc.tensor.transpose
            pe.wait_ge(S["consts"], 1)
            pe.wait_ge(S["c_silu"], 1)
            tr(P[0][:, 0:2 * KD], csil, ident[0:2 * KD, 0:2 * KD]).then_inc(S["cT_ps"], 1)

            def adaln(q, k):
                arrived(pe, ("ada", q, k))
                w = chunk(("ada", q, k))
                if (q, k) == (2, 0):
                    pe.wait_ge(S["v_sb"], NT + 1)
                for j in range(4):
                    last = mm(P[(1, 3, 2)[q]][32 * j:32 * j + 32, :], CT[:, k, :], w[:, j * HALF:(j + 1) * HALF],
                              start=(k == 0), stop=(k == KD - 1))
                last.then_inc(S["chunks_used"], 1)

            def keep_clock(n, bank):
                for _ in range(n):
                    mm(P[bank][:, 0:128], ident[:, :], ident[:, :], start=True, stop=True)

            def row_transposes(t, rows_ready, done, bank0):
                r = TILE_ROWS[t]
                pe.wait_ge(S[rows_ready], t + 1)
                for q in range(2):
                    bank = P[(bank0 + q) % 8]
                    for c in range(4):
                        last = tr(bank[:, c * 128:c * 128 + r], Ht[0:r, t, (4 * q + c) * 128:(4 * q + c + 1) * 128], ident[0:r, 0:r])
                    last.then_inc(S[done], 1)

            for t in range(NT):
                row_transposes(t, "h_rows", "hT_ps", 2 * t + 2)
            pe.wait_ge(S["cT"], 1)
            pe.wait_ge(S["hT_sb"], 2 * NT)
            for k in range(KD):
                adaln(0, k)
            pe.wait_ge(S["mod_rows"], 1)
            for c in range(4):
                last = tr(P[0][:, c * 128:(c + 1) * 128], MOD01[:, 0, c * 128:(c + 1) * 128], ident[:, :])
            last.then_inc(S["modT_ps"], 1)
            pe.wait_ge(S["ws_masked"], 1)
            for q in range(NG):
                last = tr(P[4][:, q * 128:(q + 1) * 128], WS[:, q * 128:(q + 1) * 128], ident[:, :])
            last.then_inc(S["wsT_ps"], 1)
            pe.wait_ge(S["hist_loaded"], 16)
            for q in range(NG):
                last = tr(P[5][:, q * HIST:(q + 1) * HIST], hist[:, q * 128:(q + 1) * 128], ident[0:HIST, 0:HIST])
            last.then_inc(S["histT_ps"], 1)
            pe.wait_ge(S["spool_loaded"], 16)
            tr(P[6][:, 0:NG], spr, ident[0:NG, 0:NG]).then_inc(S["spoolT_ps"], 1)

            def columns(bank, name, off):
                w = chunk(name)
                for k in range(KD):
                    last = mm(P[bank][:, 0:TOK], w[:, k, off:off + 128], hT[:, k, :], start=(k == 0), stop=(k == KD - 1))
                return last

            def ada_pieces(c):
                for q, k in ada_after[c]:
                    adaln(q, k)

            for c in range(2):
                arrived(pe, ("in", 4 + c))
                w = chunk(("in", 4 + c))
                for t in range(NT - 1):
                    for k in range(KD):
                        pe.wait_ge(S["h_cols"], 2 * KD if t or c else 2 * k + 2)
                        mm(P[t][:, c * 256:(c + 1) * 256], hT[:, k, TILE_AT[t]:TILE_AT[t] + 128], w[:, k, :],
                           start=(k == 0), stop=(k == KD - 1))
            for k in range(KD):
                for c in range(2):
                    last = mm(P[2][64 * c:64 * c + 64, 0:256], hT[:, k, TILE_AT[2]:TOK], chunk(("in", 4 + c))[:, k, :],
                              start=(k == 0), stop=(k == KD - 1))
            last.then_inc(S["chunks_used"], 2)
            ada_pieces(5)
            pe.wait_ge(S["vec_loaded"], 48)
            pe.wait_ge(S["v_sb"], 2)
            mm(P[0][:, :], ones[96:97, :], gv_row, start=True, stop=True)
            mm(P[1][:, :], ones[96:97, :], bv_row, start=True, stop=True).then_inc(S["gv_ps"], 1)
            pe.wait_ge(S["wsT"], 1)
            pe.wait_ge(S["hist_in"], 1)
            pe.wait_ge(S["spool"], 1)
            for q in range(NG):
                name = ("in", q // 2)
                arrived(pe, name)
                last = columns(4 + q, name, (q % 2) * 128)
                if q % 2:
                    last.then_inc(S["chunks_used"], 1)
                    ada_pieces(q // 2)

            def pooled():
                pe.wait_ge(S["wp_loaded"], 16)
                pe.wait_ge(S["v_rows"], NT)
                for q in range(NG):
                    pe.wait_ge(S["dT_sb"], q + 1)
                    if q >= 2:
                        pe.wait_ge(S["ya_sb"], q - 1)
                    mm(P[q % 2][:, 0:TOK], WP[:, q, :], dT[:, q, :], start=True, stop=True).then_inc(S["ya_ps"], 1)

            def last_rows_of_a():
                pe.wait_ge(S["ya_sb"], NG)
                for s, c0 in enumerate((P_AT + 256 - HIST, S_AT + 64 - HIST)):
                    for q in range(NG):
                        last = mm(P[s][0:HIST, q * 128:(q + 1) * 128], EXT[:, q, c0:c0 + HIST], ident[:, :], start=True, stop=True)
                    last.then_inc(S["st_ps"], 1)

            def spatial(q):
                for t, r in enumerate(TILE_ROWS):
                    out = P[4 + q][:, TILE_AT[t]:TILE_AT[t] + r]
                    mm(out, ones[96:97, :], bs_row[:, q * 128:q * 128 + r], start=True, stop=False)
                    last = mm(out, V[0:r, t, q * 128:(q + 1) * 128], WST[0:r, q, 0:r], start=False, stop=True)
                last.then_inc(S["s_ps"], 1)

            for q in range(NG):
                name = ("in", 2 + q // 2)
                arrived(pe, name)
                pe.wait_ge(S["a_sb"], q + 1)
                last = columns(4 + q, name, (q % 2) * 128)
                if q % 2:
                    last.then_inc(S["chunks_used"], 1)
                    ada_pieces(2 + q // 2)
                if q == 1:
                    pooled()
                if q % 2:
                    pe.wait_ge(S["u_sb"], q + 1)
                    if q == 3:
                        last_rows_of_a()
                    spatial(q - 1)
                    spatial(q)
            pe.wait_ge(S["st_sb"], 2)
            pe.wait_ge(S["mod_rows"], 3)
            for n in range(KD):
                h, bank = n // 4, 4 * (n % 2)
                if n >= 2:
                    pe.wait_ge(S["mix_sb"], n - 1)
                for name, to, rhs, pieces, off in (
                    (("in", 6 + n // 2), bank + 2, hT, KD, (n % 2) * 128), (("in", 10 + n // 2), bank + 3, hT, KD, (n % 2) * 128),
                    (("pa", h), bank, yaT, NG, (n % 4) * 128), (("pb", h), bank + 1, ybT, NG, (n % 4) * 128),
                ):
                    arrived(pe, name)
                    if name == ("pb", 0):
                        pe.wait_ge(S["yb_sb"], NG)
                    w = chunk(name)
                    for k in range(pieces):
                        last = mm(P[to][:, 0:TOK], w[:, k, off:off + 128], rhs[:, k, :], start=(k == 0), stop=(k == pieces - 1))
                        if n in (2, 4, 6) and to == bank + 2 and k == 0:
                            last.then_inc(S["chunks_used"], 4 if n == 4 else 2)
                last.then_inc(S["mix_ps"], 1)

            def w_o_product(t):
                r = TILE_ROWS[t]
                for c in range(4):
                    arrived(pe, ("wo", c))
                    w = chunk(("wo", c))
                    for k in range(2):
                        if t == 0:
                            pe.wait_ge(S["mix_sb"], max(2 * c + k + 1, KD - 1))
                        for h in range(2):
                            last = mm(o_bank(t, h), mT[:, 2 * c + k, TILE_AT[t]:TILE_AT[t] + r],
                                      w[:, k, h * HALF:(h + 1) * HALF], start=(c + k == 0), stop=(c + k == 4))
                            if t == 0 and c + k + h == 0:
                                last.then_inc(S["chunks_used"], 4)
                    if t == NT - 1:
                        last.then_inc(S["chunks_used"], 1)
                if t < NT - 1:
                    last.then_inc(S["o_ps"], 1)

            def router(t):
                r = TILE_ROWS[t]
                pe.wait_ge(S["h2T_sb"], 2 * t + 2)
                for k in range(KD):
                    last = mm(P[(6, 7, 0)[t]][0:r, 0:E], h2T[:, k, 0:r], WR[:, k, :], start=(k == 0), stop=(k == KD - 1))
                last.then_inc(S["log_ps"], 1)
            pe.wait_ge(S["wr_loaded"], 16)
            w_o_product(0)
            w_o_product(1)
            row_transposes(0, "h2_rows", "h2T_ps", 6)
            w_o_product(2)
            keep_clock(12, 5)
            router(0)
            row_transposes(1, "h2_rows", "h2T_ps", 0)
            keep_clock(5, 5)
            router(1)
            row_transposes(2, "h2_rows", "h2T_ps", 2)
            router(2)
            keep_clock(4, 5)
            pe.wait_ge(S["chosen_sb"], NT)
            pe.wait_ge(S["consts"], 3)
            for t in range(NT + 1):
                for u in range(min(t + 1, NT)):
                    last = mm(P[1][:, t * E:(t + 1) * E], (before if u == t else onesb)[:, :], chosen[:, u, :],
                              start=(u == 0), stop=(u == min(t, NT - 1)))
            last.then_inc(S["rank_ps"], 1)

            def gather():
                for t in range(NT):
                    for j in range(NQ):
                        last = mm(P[2][j * BLK:(j + 1) * BLK, 0:QW], sel[:, t, :], Ht[:, t, j * QW:(j + 1) * QW],
                                  start=(t == 0), stop=(t == NT - 1))
                last.then_inc(S["xg_ps"], 1)

            def transposes(bank, src, done):
                for c in range(PQ):
                    last = tr(P[bank][:, c * 128:(c + 1) * 128], src[:, c * 128:(c + 1) * 128], ident[:, :])
                last.then_inc(S[done], 1)

            keep_clock(18, 5)
            pe.wait_ge(S["sel_ready"], 1)
            gather()
            pe.wait_ge(S["xg_sb"], 1)
            transposes(3, xg, "xt_ps")
            pe.wait_ge(S["bias_split"], 1)

            def body(b, i, p, last_block):
                pe.wait_ge(S["xt_sb"], b)
                for k in range(KD):
                    s = 8 * p + k
                    pe.wait_ge(up_full[s], i * 16 + 16 * (mixer_uses[s] + 1))
                    for half in range(2):
                        for j in range(NQ):
                            c0 = half * D + j * QW
                            last = mm(P[half][j * BLK:(j + 1) * BLK, 0:QW], xT_blk[:, k % PQ, k // PQ, :],
                                      up_slot(s)[:, c0:c0 + QW], start=(k == 0), stop=False)
                    if last_block:
                        last.then_inc(S["chunks_used"], 1)
                pe.wait_ge(S["one_hot_e"], i * 2 + (p + 1))
                for half in range(2):
                    for j in range(NQ):
                        c0 = half * D + j * QW
                        last = mm(P[half][j * BLK:(j + 1) * BLK, 0:QW], onehot_e[:, p, :], B3[0:96, c0:c0 + QW],
                                  start=False, stop=True)
                last.then_inc(S["up_done"], 1)
                pe.wait_ge(S["sel_ready"], b + 1)
                gather()
                pe.wait_ge(S["act_sb"], b)
                transposes(4, zg, "at_ps")
                pe.wait_ge(S["at_sb"], b)
                pe.wait_ge(S["y_sb"], b)
                for k in range(KD):
                    if k == 4:
                        pe.wait_ge(S["xg_sb"], b + 1)
                        transposes(3, xg, "xt_ps")
                    pe.wait_ge(dn_full[k // 2], i * 32 + 16 * (p + 1))
                    w = dn_slot(k // 2)
                    for j in range(NQ):
                        last = mm(P[5][j * BLK:(j + 1) * BLK, 0:QW], aT_blk[:, k % PQ, k // PQ, :],
                                  w[:, k % 2, j * QW:(j + 1) * QW], start=(k == 0), stop=False)
                    if last_block and k % 2:
                        last.then_inc(S["down_used"], 1)
                for j in range(NQ):
                    last = mm(P[5][j * BLK:(j + 1) * BLK, 0:QW], onehot_e[:, p, :], B3[0:96, F2 + j * QW:F2 + (j + 1) * QW],
                              start=False, stop=True)
                last.then_inc(S["y_ps"], 1)
            expert_blocks(pe, body)
            for s in range(2):
                for h in range(2):
                    rows = slice(32 * (2 + h), 32 * (3 + h))
                    last = mm(P[(6, 0)[s] + h][:, :], pick[rows, s, :], MODF[rows, :], start=True, stop=True)
            last.then_inc(S["gf_ps"], 1)
            pe.wait_ge(S["diagonals"], TOPK)
            keep_clock(60, 4)
            pe.wait_ge(gathered[1], 16 * TOPK)
            for k in range(TOPK):
                for h in range(2):
                    last = mm(P[2 + h][:, :], diag[:, k, :], G[:, 1, k, h * HALF:(h + 1) * HALF], start=(k == 0), stop=(k == TOPK - 1))
            last.then_inc(S["f1_ps"], 1)


_INS = ["x_prompt", "x_sample", "cache_pool", "c_prompt", "c_sample", "w_ada", "b_ada", "g_pre_mix", "g_post_mix",
        "g_pre_ffn", "g_post_ffn", "w_in", "w_pool", "s_pool", "g_v", "b_v", "w_s", "b_s", "p_a", "p_b", "w_o",
        "w_router", "b_router", "w_up", "b_up", "w_down", "b_down"]


def kernel(**inputs):
    import numpy as _np
    import concourse.bacc as _bacc
    from concourse import mybir as _mybir
    from concourse.bass_utils import run_bass_kernel_spmd as _run

    nc = _bacc.Bacc("TRN2", target_bir_lowering=False, num_devices=1)
    arrays, args = {}, []
    for name in _INS:
        a = _np.ascontiguousarray(inputs[name])
        arrays[f"in_{name}_dram"] = a
        args.append(nc.dram_tensor(f"in_{name}_dram", a.shape, _mybir.dt.from_np(a.dtype), kind="ExternalInput").ap())
    xp, xs, cache = (inputs[n].shape for n in ("x_prompt", "x_sample", "cache_pool"))
    outs = [xp, xs, (cache[0], xp[0], cache[2], cache[3]), cache, (cache[0], xs[0], xs[1], inputs["g_v"].shape[1])]
    for i, shape in enumerate(outs):
        args.append(nc.dram_tensor(f"out_{i}_dram", shape, _mybir.dt.from_np(_np.dtype("float32")), kind="ExternalOutput").ap())
    pool_gmlp_moe_streaming_step_kernel(nc, *args)
    r = _run(nc, [arrays], core_ids=[0])
    return tuple(r.results[0][f"out_{i}_dram"] for i in range(len(outs)))
```
